# Optimizing a Trainium2 kernel written in Bass

```python
import jax, jax.numpy as jnp
from jax import lax
import numpy as np

D_MODEL = 1024
BATCH = 1
SEQ = 1024
DEPTH = 1

GRID_W = 64
CTX_LEN = 256
D_MIX = D_MODEL
D_ATTN = D_MIX // 2
D_POOL = D_MIX - D_ATTN
MLA_HEADS = 4
QK_NOPE_DIM = 128
QK_ROPE_DIM = 64
QK_HEAD_DIM = QK_NOPE_DIM + QK_ROPE_DIM
V_HEAD_DIM = D_ATTN // MLA_HEADS
Q_LORA_RANK = 256
KV_LORA_RANK = 128
ROPE_AXIS_DIM = QK_ROPE_DIM // 2
ROPE_BASE = 10000.0
POOL_WINDOWS = (2, 4, 8, 16)
POOL_GROUPS = len(POOL_WINDOWS)
POOL_GROUP_DIM = D_POOL // POOL_GROUPS
Q_BLOCK = 128
NORM_EPS = 1e-6

OFF_CQ = 0
OFF_CKV = OFF_CQ + Q_LORA_RANK
OFF_KR = OFF_CKV + KV_LORA_RANK
OFF_GA = OFF_KR + QK_ROPE_DIM
OFF_PIN = OFF_GA + D_ATTN
OFF_GP = OFF_PIN + D_POOL
D_IN_PROJ = OFF_GP + D_POOL


def _rms(x, g):
    xf = x.astype(jnp.float32)
    y = xf * lax.rsqrt(jnp.mean(xf * xf, axis=-1, keepdims=True) + NORM_EPS)
    return (y * g.astype(jnp.float32)).astype(x.dtype)

def _rotate_half(x):
    x1, x2 = jnp.split(x, 2, axis=-1)
    return jnp.concatenate([-x2, x1], axis=-1)

def _axial_rope_tables(L):
    rows = L // GRID_W
    row = jnp.repeat(jnp.arange(rows, dtype=jnp.float32), GRID_W)
    col = jnp.tile(jnp.arange(GRID_W, dtype=jnp.float32), rows)
    n_freq = ROPE_AXIS_DIM // 2
    inv = ROPE_BASE ** (-jnp.arange(n_freq, dtype=jnp.float32) / n_freq)
    ang_r = row[:, None] * inv
    ang_c = col[:, None] * inv
    ang = jnp.concatenate([ang_r, ang_r, ang_c, ang_c], axis=-1)
    return jnp.cos(ang), jnp.sin(ang)

def _apply_axial_rope(x, cos, sin):
    xr, xc = jnp.split(x, 2, axis=-1)
    rot = jnp.concatenate([_rotate_half(xr), _rotate_half(xc)], axis=-1)
    c = cos[:, None, :]
    s = sin[:, None, :]
    return (x.astype(jnp.float32) * c + rot.astype(jnp.float32) * s).astype(x.dtype)

def _mla_qkv(u, q_lora_g, w_uq, kv_lora_g, w_ukv, q_norm_g, k_norm_g, rope):
    B, L = u.shape[0], u.shape[1]
    cq = u[..., OFF_CQ:OFF_CKV]
    ckv = u[..., OFF_CKV:OFF_KR]
    k_rope = u[..., OFF_KR:OFF_GA]
    q = (_rms(cq, q_lora_g) @ w_uq).reshape(B, L, MLA_HEADS, QK_HEAD_DIM)
    kv = (_rms(ckv, kv_lora_g) @ w_ukv).reshape(B, L, MLA_HEADS, QK_NOPE_DIM + V_HEAD_DIM)
    k_nope, v = kv[..., :QK_NOPE_DIM], kv[..., QK_NOPE_DIM:]
    k = jnp.concatenate(
        [k_nope, jnp.broadcast_to(k_rope[:, :, None, :], (B, L, MLA_HEADS, QK_ROPE_DIM))], axis=-1)
    q = _rms(q, q_norm_g)
    k = _rms(k, k_norm_g)
    if rope is not None:
        cos, sin = rope
        q = jnp.concatenate([q[..., :QK_NOPE_DIM], _apply_axial_rope(q[..., QK_NOPE_DIM:], cos, sin)], axis=-1)
        k = jnp.concatenate([k[..., :QK_NOPE_DIM], _apply_axial_rope(k[..., QK_NOPE_DIM:], cos, sin)], axis=-1)
    tr = lambda t: jnp.transpose(t, (0, 2, 1, 3))
    return tr(q), tr(k), tr(v)

def _attend(q, k, v):
    B, H, Lq, dk = q.shape
    nb = Lq // Q_BLOCK
    scale = QK_HEAD_DIM ** -0.5
    qb = jnp.transpose(q.reshape(B, H, nb, Q_BLOCK, dk), (2, 0, 1, 3, 4))

    def one(qblk):
        s = jnp.einsum('bhqd,bhkd->bhqk', qblk, k).astype(jnp.float32) * scale
        p = jax.nn.softmax(s, axis=-1)
        return jnp.einsum('bhqk,bhkd->bhqd', p.astype(v.dtype), v)

    o = lax.map(one, qb)
    o = jnp.transpose(o, (1, 3, 0, 2, 4)).reshape(B, Lq, H * v.shape[-1])
    return o

def _multiscale_pool(u, w_pool, pool_scale):
    B, L, _ = u.shape
    ug = u.reshape(B, L, POOL_GROUPS, POOL_GROUP_DIM)
    cs = jnp.concatenate(
        [jnp.zeros((B, 1, POOL_GROUPS, POOL_GROUP_DIM), jnp.float32),
         jnp.cumsum(ug.astype(jnp.float32), axis=1)], axis=1)
    t = jnp.arange(L, dtype=jnp.int32)[:, None]
    w = jnp.array(POOL_WINDOWS, dtype=jnp.int32)[None, :]
    lo = jnp.clip(t - w // 2, 0, L)
    hi = jnp.clip(t - w // 2 + w, 0, L)
    g = jnp.arange(POOL_GROUPS, dtype=jnp.int32)[None, :]
    win_sum = cs[:, hi, g, :] - cs[:, lo, g, :]
    cnt = (hi - lo).astype(jnp.float32)[None, :, :, None]
    pooled = (win_sum / cnt - ug.astype(jnp.float32)).astype(u.dtype)
    y = jnp.einsum('blgc,gcd->blgd', pooled, w_pool).reshape(B, L, D_POOL)
    return y * pool_scale

def _branches(u, mla_out, w_pool, pool_scale):
    gate_a = u[..., OFF_GA:OFF_PIN]
    pool_in = u[..., OFF_PIN:OFF_GP]
    gate_p = u[..., OFF_GP:D_IN_PROJ]
    br_a = jax.nn.silu(gate_a) * mla_out
    br_p = jax.nn.silu(gate_p) * _multiscale_pool(pool_in, w_pool, pool_scale)
    return jnp.concatenate([br_a, br_p], axis=-1)

def first_inputs(seed: int = 0) -> dict:
    key = jax.random.key(seed)
    ks = jax.random.split(key, 20)
    f32 = jnp.float32
    nrm = lambda k, shape, s: jax.random.normal(k, shape, f32) * s
    return {
        "x": nrm(ks[0], (BATCH, SEQ, D_MODEL), 1.0),
        "c": nrm(ks[1], (BATCH, D_MODEL), 1.0),
        "ctx": nrm(ks[2], (BATCH, CTX_LEN, D_MODEL), 1.0),
        "c_ctx": nrm(ks[3], (D_MODEL,), 1.0),
        "w_mod": nrm(ks[4], (DEPTH, D_MODEL, 3 * D_MODEL), 0.5 * D_MODEL ** -0.5),
        "b_mod": nrm(ks[5], (DEPTH, 3 * D_MODEL), 0.02),
        "norm_g": 1.0 + nrm(ks[6], (DEPTH, D_MODEL), 0.1),
        "w_in": nrm(ks[7], (DEPTH, D_MODEL, D_IN_PROJ), D_MODEL ** -0.5),
        "q_lora_g": 1.0 + nrm(ks[8], (DEPTH, Q_LORA_RANK), 0.1),
        "w_uq": nrm(ks[9], (DEPTH, Q_LORA_RANK, MLA_HEADS * QK_HEAD_DIM), Q_LORA_RANK ** -0.5),
        "kv_lora_g": 1.0 + nrm(ks[10], (DEPTH, KV_LORA_RANK), 0.1),
        "w_ukv": nrm(ks[11], (DEPTH, KV_LORA_RANK, MLA_HEADS * (QK_NOPE_DIM + V_HEAD_DIM)), KV_LORA_RANK ** -0.5),
        "q_norm_g": 1.0 + nrm(ks[12], (DEPTH, QK_HEAD_DIM), 0.1),
        "k_norm_g": 1.0 + nrm(ks[13], (DEPTH, QK_HEAD_DIM), 0.1),
        "w_pool": nrm(ks[14], (DEPTH, POOL_GROUPS, POOL_GROUP_DIM, POOL_GROUP_DIM), POOL_GROUP_DIM ** -0.5),
        "pool_scale": 1.0 + nrm(ks[15], (DEPTH, D_POOL), 0.1),
        "w_out": nrm(ks[16], (DEPTH, D_MIX, D_MODEL), D_MIX ** -0.5),
    }

def first_block(x, c, ctx, c_ctx, w_mod, b_mod, norm_g, w_in, q_lora_g, w_uq, kv_lora_g, w_ukv,
              q_norm_g, k_norm_g, w_pool, pool_scale, w_out):
    L = x.shape[1]
    rope = _axial_rope_tables(L)
    for l in range(DEPTH):
        mod = jax.nn.silu(c) @ w_mod[l] + b_mod[l]
        shift, scale, gate = jnp.split(mod, 3, axis=-1)
        mod_c = jax.nn.silu(c_ctx) @ w_mod[l] + b_mod[l]
        shift_c, scale_c, gate_c = jnp.split(mod_c, 3, axis=-1)

        h = _rms(x, norm_g[l]) * (1.0 + scale[:, None, :]) + shift[:, None, :]
        hc = _rms(ctx, norm_g[l]) * (1.0 + scale_c) + shift_c
        u = h @ w_in[l]
        uc = hc @ w_in[l]

        q, k, v = _mla_qkv(u, q_lora_g[l], w_uq[l], kv_lora_g[l], w_ukv[l],
                           q_norm_g[l], k_norm_g[l], rope)
        qc, kc, vc = _mla_qkv(uc, q_lora_g[l], w_uq[l], kv_lora_g[l], w_ukv[l],
                              q_norm_g[l], k_norm_g[l], None)
        k_all = jnp.concatenate([kc, k], axis=2)
        v_all = jnp.concatenate([vc, v], axis=2)
        attn = _attend(q, k_all, v_all)
        y = _branches(u, attn, w_pool[l], pool_scale[l]) @ w_out[l]
        x_new = x + gate[:, None, :] * y

        if l < DEPTH - 1:
            attn_c = _attend(qc, kc, vc)
            yc = _branches(uc, attn_c, w_pool[l], pool_scale[l]) @ w_out[l]
            ctx = ctx + gate_c * yc
        x = x_new
    return x


DEPTH_2 = 2

N_EVEN = (DEPTH_2 + 1) // 2
N_ODD = DEPTH_2 // 2
CHUNK = 64
EPS = 1e-6
RET_HEADS = 4
RET_DV = D_MODEL // 2 // RET_HEADS
RET_DK = RET_DV
GLA_HEADS = 4
GLA_DV = D_MODEL // 2 // GLA_HEADS
GLA_DK = GLA_DV // 2
GLA_RANK = 16
GLA_TAU = 16.0
AB_SIZES = (RET_HEADS * RET_DK, RET_HEADS * RET_DK, RET_HEADS * RET_DV, RET_HEADS * RET_DV,
            GLA_HEADS * GLA_DK, GLA_HEADS * GLA_DK, GLA_HEADS * GLA_DV, GLA_HEADS * GLA_DV,
            GLA_RANK)
AB_IN = sum(AB_SIZES)
HGRN_DK = 128
HGRN_HEADS = D_MODEL // HGRN_DK
HGRN_DV = D_MODEL // HGRN_HEADS
C_IN = 4 * D_MODEL
D_FF = ((8 * D_MODEL // 3 + 255) // 256) * 256
N_EXPERTS = 8
TOP_K = 2
EXPERT_FF = 7 * D_MODEL // 2
OUT_SCALE = (2 * DEPTH_2) ** -0.5


def rms_norm(x, g):
    xf = x.astype(jnp.float32)
    y = xf * lax.rsqrt(jnp.mean(xf * xf, axis=-1, keepdims=True) + EPS)
    return (y * g.astype(jnp.float32)).astype(x.dtype)

def rotary(x, positions):
    d = x.shape[-1]
    inv_freq = ROPE_BASE ** (-jnp.arange(0, d, 2, dtype=jnp.float32) / d)
    ang = positions.astype(jnp.float32)[..., None, None] * inv_freq
    cos, sin = jnp.cos(ang), jnp.sin(ang)
    xf = x.astype(jnp.float32)
    x1, x2 = xf[..., : d // 2], xf[..., d // 2:]
    return jnp.concatenate([x1 * cos - x2 * sin, x2 * cos + x1 * sin], axis=-1)

def _to_chunks(a):
    b, t, h, d = a.shape
    return a.reshape(b, t // CHUNK, CHUNK, h, d).transpose(1, 0, 3, 2, 4)

def _from_chunks(a):
    nc, b, h, c, d = a.shape
    return a.transpose(1, 0, 3, 2, 4).reshape(b, nc * c, h, d)

def _causal_mask():
    t = jnp.arange(CHUNK)
    return t[:, None] >= t[None, :]

def retention_chunkwise(q, k, v, log_gamma):
    b, _, h, dk = q.shape
    dv = v.shape[-1]
    t = jnp.arange(CHUNK, dtype=jnp.float32)
    lg = log_gamma.astype(jnp.float32)
    rel = t[:, None] - t[None, :]
    intra_decay = jnp.exp(jnp.where(_causal_mask()[None], rel[None] * lg[:, None, None], -jnp.inf))
    q_decay = jnp.exp((t[None, :] + 1.0) * lg[:, None])[..., None]
    k_decay = jnp.exp((CHUNK - 1.0 - t[None, :]) * lg[:, None])[..., None]
    chunk_decay = jnp.exp(CHUNK * lg)[:, None, None]

    def step(state, inp):
        qc, kc, vc = inp
        scores = jnp.einsum('bhid,bhjd->bhij', qc, kc) * intra_decay
        o = (jnp.einsum('bhij,bhjv->bhiv', scores, vc)
             + jnp.einsum('bhid,bhdv->bhiv', qc * q_decay, state))
        state = chunk_decay * state + jnp.einsum('bhjd,bhjv->bhdv', kc * k_decay, vc)
        return state, o

    s0 = jnp.zeros((b, h, dk, dv), jnp.float32)
    _, o = lax.scan(step, s0, (_to_chunks(q), _to_chunks(k), _to_chunks(v)))
    return _from_chunks(o)

def gated_chunkwise(q, k, v, log_f):
    b, _, h, dk = q.shape
    dv = v.shape[-1]
    mask = _causal_mask()[:, :, None]
    g_cum = jnp.cumsum(_to_chunks(log_f), axis=-2)

    def step(state, inp):
        qc, kc, vc, gc = inp
        diff = gc[:, :, :, None, :] - gc[:, :, None, :, :]
        decay = jnp.exp(jnp.where(mask, diff, -jnp.inf))
        scores = jnp.einsum('bhid,bhjd,bhijd->bhij', qc, kc, decay)
        g_last = gc[:, :, -1:, :]
        o = (jnp.einsum('bhij,bhjv->bhiv', scores, vc)
             + jnp.einsum('bhid,bhdv->bhiv', qc * jnp.exp(gc), state))
        state = (jnp.exp(g_last[:, :, 0, :])[..., None] * state
                 + jnp.einsum('bhjd,bhjv->bhdv', kc * jnp.exp(g_last - gc), vc))
        return state, o

    s0 = jnp.zeros((b, h, dk, dv), jnp.float32)
    _, o = lax.scan(step, s0, (_to_chunks(q), _to_chunks(k), _to_chunks(v), g_cum))
    return _from_chunks(o)

def retnet_gla_mixer(h, positions, w_in, w_a2, b_a2, ret_g, gla_g, w_out):
    b, t, _ = h.shape
    z = h @ w_in
    aq, ak, av, ag, bq, bk, bv, bg, ba = jnp.split(z, np.cumsum(AB_SIZES)[:-1], axis=-1)
    f32 = jnp.float32

    def heads(a, n):
        return a.reshape(b, t, n, -1).astype(f32)

    qa = rotary(heads(aq, RET_HEADS), positions)
    ka = rotary(heads(ak, RET_HEADS), positions) * (RET_DK ** -0.5)
    log_gamma = jnp.log1p(-jnp.exp2(-5.0 - jnp.arange(RET_HEADS, dtype=f32)))
    oa = retention_chunkwise(qa, ka, heads(av, RET_HEADS), log_gamma)
    oa = rms_norm(oa, ret_g) * jax.nn.silu(heads(ag, RET_HEADS))
    log_alpha = jax.nn.log_sigmoid((ba @ w_a2 + b_a2).astype(f32)) / GLA_TAU
    ob = gated_chunkwise(heads(bq, GLA_HEADS) * (GLA_DK ** -0.5), heads(bk, GLA_HEADS),
                         heads(bv, GLA_HEADS), heads(log_alpha, GLA_HEADS))
    ob = rms_norm(ob, gla_g) * jax.nn.silu(heads(bg, GLA_HEADS))
    o = jnp.concatenate([oa.reshape(b, t, -1), ob.reshape(b, t, -1)], axis=-1)
    return o.astype(h.dtype) @ w_out

def hgrn2_mixer(h, lb, w_in, norm_g, w_out):
    b, t, d = h.shape
    f32 = jnp.float32
    q, f, i, g = jnp.split(h @ w_in, 4, axis=-1)

    def heads(a):
        return a.reshape(b, t, HGRN_HEADS, -1).astype(f32)

    f = heads(f)
    lb = lb.astype(f32)
    log_f = jnp.logaddexp(jnp.log(lb), jnp.log1p(-lb) + jax.nn.log_sigmoid(f))
    k = (1.0 - lb) * jax.nn.sigmoid(-f)
    qh = jax.nn.silu(heads(q)) * (HGRN_DK ** -0.5)
    o = gated_chunkwise(qh, k, heads(i), log_f)
    o = rms_norm(o, norm_g) * jax.nn.silu(heads(g))
    return o.reshape(b, t, d).astype(h.dtype) @ w_out

def swiglu(h, w_gate, w_up, w_down):
    return (jax.nn.silu(h @ w_gate) * (h @ w_up)) @ w_down

def moe_swiglu(h, w_router, w_gate, w_up, w_down):
    b, t, d = h.shape
    xt = h.reshape(b * t, d)
    logits = (xt @ w_router).astype(jnp.float32)
    top_logits, top_idx = lax.top_k(logits, TOP_K)
    gates = jax.nn.softmax(top_logits, axis=-1)
    flat_e = top_idx.reshape(-1)
    order = jnp.argsort(flat_e)
    group_sizes = jnp.bincount(flat_e, length=N_EXPERTS).astype(jnp.int32)
    xs = xt[order // TOP_K]
    hid = (jax.nn.silu(lax.ragged_dot(xs, w_gate, group_sizes))
           * lax.ragged_dot(xs, w_up, group_sizes))
    ys = lax.ragged_dot(hid, w_down, group_sizes)
    y = jnp.zeros_like(ys).at[order].set(ys).reshape(b * t, TOP_K, d)
    out = jnp.einsum('nk,nkd->nd', gates.astype(y.dtype), y)
    return out.reshape(b, t, d)

def second_inputs(seed: int = 0) -> dict:
    key = jax.random.key(seed)
    ks = jax.random.split(key, 24)
    f32 = jnp.float32

    def nrm(k, shape, scale):
        return jax.random.normal(k, shape, f32) * scale

    def gain(k, shape):
        return 1.0 + 0.02 * jax.random.normal(k, shape, f32)

    ds = D_MODEL ** -0.5
    return {
        "x": nrm(ks[0], (BATCH, SEQ, D_MODEL), 1.0),
        "positions": jnp.broadcast_to(jnp.arange(SEQ, dtype=jnp.int32), (BATCH, SEQ)),
        "norm_mix_g": gain(ks[1], (DEPTH_2, D_MODEL)),
        "norm_ffn_g": gain(ks[2], (DEPTH_2, D_MODEL)),
        "final_norm_g": gain(ks[3], (D_MODEL,)),
        "ab_w_in": nrm(ks[4], (N_EVEN, D_MODEL, AB_IN), ds),
        "gla_w_a2": nrm(ks[5], (N_EVEN, GLA_RANK, GLA_HEADS * GLA_DK), GLA_RANK ** -0.5),
        "gla_b_a2": nrm(ks[6], (N_EVEN, GLA_HEADS * GLA_DK), 0.1),
        "ret_norm_g": gain(ks[7], (N_EVEN, RET_DV)),
        "gla_norm_g": gain(ks[8], (N_EVEN, GLA_DV)),
        "ab_w_out": nrm(ks[9], (N_EVEN, D_MODEL, D_MODEL), ds * OUT_SCALE),
        "ffn_w_gate": nrm(ks[10], (N_EVEN, D_MODEL, D_FF), ds),
        "ffn_w_up": nrm(ks[11], (N_EVEN, D_MODEL, D_FF), ds),
        "ffn_w_down": nrm(ks[12], (N_EVEN, D_FF, D_MODEL), D_FF ** -0.5 * OUT_SCALE),
        "hgrn_lb_logits": nrm(ks[13], (DEPTH_2, HGRN_HEADS * HGRN_DK), 0.1),
        "c_w_in": nrm(ks[14], (N_ODD, D_MODEL, C_IN), ds),
        "hgrn_norm_g": gain(ks[15], (N_ODD, HGRN_DV)),
        "c_w_out": nrm(ks[16], (N_ODD, D_MODEL, D_MODEL), ds * OUT_SCALE),
        "moe_router": nrm(ks[17], (N_ODD, D_MODEL, N_EXPERTS), ds),
        "moe_w_gate": nrm(ks[18], (N_ODD, N_EXPERTS, D_MODEL, EXPERT_FF), ds),
        "moe_w_up": nrm(ks[19], (N_ODD, N_EXPERTS, D_MODEL, EXPERT_FF), ds),
        "moe_w_down": nrm(ks[20], (N_ODD, N_EXPERTS, EXPERT_FF, D_MODEL), EXPERT_FF ** -0.5 * OUT_SCALE),
    }

def second_block(x, positions, norm_mix_g, norm_ffn_g, final_norm_g, ab_w_in, gla_w_a2, gla_b_a2,
              ret_norm_g, gla_norm_g, ab_w_out, ffn_w_gate, ffn_w_up, ffn_w_down,
              hgrn_lb_logits, c_w_in, hgrn_norm_g, c_w_out, moe_router, moe_w_gate,
              moe_w_up, moe_w_down):
    lb_cum = jnp.cumsum(jax.nn.softmax(hgrn_lb_logits.astype(jnp.float32), axis=0), axis=0)
    lower_bounds = lb_cum - lb_cum[0:1]
    h = x
    for l in range(DEPTH_2):
        e = l // 2
        hn = rms_norm(h, norm_mix_g[l])
        if l % 2 == 0:
            h = h + retnet_gla_mixer(hn, positions, ab_w_in[e], gla_w_a2[e], gla_b_a2[e],
                                     ret_norm_g[e], gla_norm_g[e], ab_w_out[e])
            h = h + swiglu(rms_norm(h, norm_ffn_g[l]), ffn_w_gate[e], ffn_w_up[e], ffn_w_down[e])
        else:
            lb = lower_bounds[l].reshape(HGRN_HEADS, HGRN_DK)
            h = h + hgrn2_mixer(hn, lb, c_w_in[e], hgrn_norm_g[e], c_w_out[e])
            h = h + moe_swiglu(rms_norm(h, norm_ffn_g[l]), moe_router[e], moe_w_gate[e],
                               moe_w_up[e], moe_w_down[e])
    return rms_norm(h, final_norm_g)


def setup_inputs(seed=0):
    out = dict(first_inputs(seed))
    for name, value in second_inputs(seed + 1).items():
        if name != "x":
            out[name + "_2"] = value
    return out


def reference(
    x, c, ctx, c_ctx, w_mod, b_mod, norm_g, w_in, q_lora_g, w_uq, kv_lora_g, w_ukv, q_norm_g,
    k_norm_g, w_pool, pool_scale, w_out, positions_2, norm_mix_g_2, norm_ffn_g_2,
    final_norm_g_2, ab_w_in_2, gla_w_a2_2, gla_b_a2_2, ret_norm_g_2, gla_norm_g_2, ab_w_out_2,
    ffn_w_gate_2, ffn_w_up_2, ffn_w_down_2, hgrn_lb_logits_2, c_w_in_2, hgrn_norm_g_2,
    c_w_out_2, moe_router_2, moe_w_gate_2, moe_w_up_2, moe_w_down_2,
):
    x = first_block(
        x, c, ctx, c_ctx, w_mod, b_mod, norm_g, w_in, q_lora_g, w_uq, kv_lora_g, w_ukv,
        q_norm_g, k_norm_g, w_pool, pool_scale, w_out,
    )
    return second_block(
        x, positions_2, norm_mix_g_2, norm_ffn_g_2, final_norm_g_2, ab_w_in_2, gla_w_a2_2,
        gla_b_a2_2, ret_norm_g_2, gla_norm_g_2, ab_w_out_2, ffn_w_gate_2, ffn_w_up_2,
        ffn_w_down_2, hgrn_lb_logits_2, c_w_in_2, hgrn_norm_g_2, c_w_out_2, moe_router_2,
        moe_w_gate_2, moe_w_up_2, moe_w_down_2,
    )


_drawn_inputs = setup_inputs


def setup_inputs(seed=0):
    import zlib

    import numpy as np

    out = dict(_drawn_inputs(seed))
    spreads = {}
    factors = {'ctx': 6.634,
     'c_ctx': 3.5,
     'b_mod': 3.04,
     'q_lora_g': 8.0,
     'kv_lora_g': 6.098,
     'q_norm_g': 8.0,
     'k_norm_g': 8.0,
     'pool_scale': 2.733,
     'norm_mix_g_2': 2.807,
     'norm_ffn_g_2': 7.829,
     'final_norm_g_2': 8.098,
     'gla_b_a2_2': 3.723,
     'ret_norm_g_2': 21.721,
     'gla_norm_g_2': 8.0,
     'hgrn_lb_logits_2': 7.348,
     'hgrn_norm_g_2': 24.822}
    for name, (base, spread) in spreads.items():
        noise = np.random.default_rng([zlib.crc32(name.encode()), seed]).standard_normal(out[name].shape)
        drawn = base * np.exp(spread * noise) if base else spread * noise
        out[name] = __import__('jax').numpy.asarray(drawn.astype(out[name].dtype))
    for name, factor in factors.items():
        out[name] = (out[name] * factor).astype(out[name].dtype)
    return out
```

```python
import math
from contextlib import ExitStack, contextmanager

import numpy as np
import concourse.bass as bass
from concourse import mybir

P = 128
F32 = mybir.dt.float32
I32 = mybir.dt.int32
U32 = mybir.dt.uint32
ALU = mybir.AluOpType
ACT = mybir.ActivationFunctionType
AX = mybir.AxisListType
ds = bass.ds

D = 1024
T = 1024
CTX = 256
NT = T // P
NC_T = CTX // P
KD = D // P
HEADS = 4
NOPE, ROPE = 128, 64
QK = NOPE + ROPE
LORA_Q, LORA_KV = 256, 128
LR = LORA_Q + LORA_KV + ROPE
KEYS = T + CTX
NK = KEYS // P
EPS = 1e-6
D_FF = 2816
FF_T = D_FF // P
NE = 8
E_FF = 3584
EF_T = E_FF // P
UNIT = 512
MAX_UNITS = (2 * T + NE * (UNIT - 1)) // UNIT
SLOTS = MAX_UNITS * UNIT
GRAIN = 16
LEVELS = (64, 32, 16, 8, 4, 2, 1)
NLEV = len(LEVELS) + 1
WINDOWS = (2, 4, 8, 16)
PAD = 16
VECS = 101
ZERO_W = 256
TWO_PI = 2 * math.pi


def shape_constants():
    f = np.float32
    i = np.arange(P)
    out = {"ident": np.eye(P, dtype=f)}
    n = ROPE // 4
    inv = (10000.0 ** (-np.arange(n, dtype=f) / n)).astype(f)
    row, col = np.repeat(np.arange(T // 64, dtype=f), 64), np.tile(np.arange(64, dtype=f), T // 64)
    ar, ac = row[:, None] * inv, col[:, None] * inv
    ang = np.concatenate([ar, ar, ac, ac], -1)
    sign = np.tile(np.repeat(np.array([-1, 1], f), n), 2)
    out["axial"] = np.stack([np.cos(ang), np.sin(ang) * sign]).astype(f)
    t = np.arange(T)
    out["inv_count"] = np.stack([1.0 / (np.clip(t - w // 2 + w, 0, T) - np.clip(t - w // 2, 0, T)) for w in WINDOWS]).astype(f)
    out["inv_freq"] = (10000.0 ** (-np.arange(0, P, 2, dtype=f) / P)).astype(f)
    lg = np.log1p(-np.exp2(-5.0 - np.arange(4, dtype=np.float64)))
    rel = i[None, :] - i[:, None]
    out["ret_mask"] = P ** -0.5 * np.where(rel[:, None, :] >= 0, np.exp(np.maximum(rel, 0)[:, None, :] * lg[None, :, None]), 0)
    out["ret_mask"] = out["ret_mask"].astype(f)
    out["ret_q"] = np.exp((i[None, :] + 1.0) * lg[:, None]).astype(f)
    out["ret_k"] = P ** -0.5 * np.exp((P - 1.0 - i[:, None]) * lg[None, :])
    out["ret_k"] = out["ret_k"].astype(f)
    out["ret_chunk"] = np.repeat(np.exp(P * lg), P).astype(f)
    m = [((i[:, None] // (2 * s)) == (i[None, :] // (2 * s))) & (i[:, None] % (2 * s) < s) & (i[None, :] % (2 * s) >= s) for s in LEVELS]
    m.append(i[:, None] == i[None, :])
    out["level_mask"] = np.stack(m, 1).astype(np.uint32)
    out["before"] = (i[:, None] < i[None, :]).astype(f)
    return out


@contextmanager
def stage(nc, name, *sems):
    handles = [nc.alloc_semaphore(f"{name}_{s}") for s in sems]
    with nc.Block() as block:
        yield (block, *handles)
    nc.clear_and_free_semaphores(handles)
    nc.all_engine_barrier()


class Arena:

    def __init__(self, tensor):
        self.t = tensor

    def at(self, off, *shape):
        n = math.prod(shape)
        ap = self.t[:, off:off + n]
        if len(shape) == 2:
            return ap.rearrange("p (a b) -> p a b", a=shape[0])
        if len(shape) == 3:
            return ap.rearrange("p (a b c) -> p a b c", a=shape[0], b=shape[1])
        return ap


def cols(v):
    return v.rearrange("(k p) -> p k", p=P)


def rows(v, n=P):
    return v.rearrange("(a n) -> a n", a=1).broadcast_to([n, v.shape[0]])


def credit(eng, sem, n):
    eng.nop().then_inc(sem, n)


def norm_stage(nc, g, name, src, n, eps_d, dst, scale, shift=None, rows_out=None):
    ss, sq, rs = g.small.at(0, 16), g.small.at(16, 16), g.small.at(32, 16)
    junk, xs = g.scratch.at(0, D), g.scratch.at(D, 2, D)
    with stage(nc, name, "squares", "root", "rstd", "xs", "tr", "ev", "sh", "r0", "r1") as (block, squares, root, rstd, xs_ready, tr_done, ev_done, shifted, r0, r1):
        row_out = (r0, r1)
        if rows_out is not None:
            @block.sync
            def _(sp):
                credit(sp, r0, 16)
                credit(sp, r1, 16)
                with sp.Fori(0, n // 2) as i:
                    for b in range(2):
                        sp.wait_ge(xs_ready, i * 2 + (b + 1))
                        sp.dma_start(rows_out.rearrange("(t p) d -> p t d", p=P)[:, ds(i * 2 + b, 1), :].rearrange("p a d -> p (a d)"), xs[:, b, :]).then_inc(row_out[b], 16)
                for b in range(2):
                    sp.wait_ge(row_out[b], 16 * (n // 2 + 1))

        @block.scalar
        def _(act):
            with act.Fori(0, n) as t:
                nc.scalar.activation(junk, src[:, ds(t, 1), :].rearrange("p a d -> p (a d)"), ACT.Square, accum_out=ss[:, ds(t, 1)]).then_inc(squares, 1)
                act.drain()
            nc.scalar.activation(sq[:, 0:n], ss[:, 0:n], ACT.Sqrt, scale=1.0 / D, bias=g.eps[:, 0:1]).then_inc(root, 1)

        @block.vector
        def _(dve):
            dve.wait_ge(root, 1)
            nc.vector.reciprocal(rs[:, 0:n], sq[:, 0:n]).then_inc(rstd, 1)
            with dve.Fori(0, n // 2) as i:
                for b in range(2):
                    dve.wait_ge(tr_done, i * 2 + (b + 3))
                    nc.vector.tensor_tensor(dst[:, :, ds((i * 2 + b) * P, P)],
                                            g.ps[:, 2 * b:2 * b + 2, :].rearrange("p a (k t) -> p (a k) t", t=P),
                                            scale.unsqueeze(2).broadcast_to([P, KD, P]), ALU.mult).then_inc(ev_done, 1)
                    if shift is not None:
                        dve.drain()
                        nc.vector.tensor_tensor(dst[:, :, ds((i * 2 + b) * P, P)], dst[:, :, ds((i * 2 + b) * P, P)],
                                                shift.unsqueeze(2).broadcast_to([P, KD, P]), ALU.add).then_inc(shifted, 1)

        @block.gpsimd
        def _(pool):
            credit(pool, tr_done, 2)
            pool.wait_ge(rstd, 1)
            with pool.Fori(0, n // 2) as i:
                for b in range(2):
                    pool.wait_ge(tr_done, i * 2 + (b + 1))
                    if rows_out is not None:
                        pool.wait_ge(row_out[b], i * 16 + 16)
                    nc.gpsimd.tensor_tensor(xs[:, b, :], src[:, ds(i * 2 + b, 1), :].rearrange("p a d -> p (a d)"),
                                            rs[:, ds(i * 2 + b, 1)].broadcast_to([P, D]), ALU.mult).then_inc(xs_ready, 1)

        @block.tensor
        def _(pe):
            credit(pe, ev_done, 2)
            with pe.Fori(0, n // 2) as i:
                for b in range(2):
                    pe.wait_ge(xs_ready, i * 2 + (b + 1))
                    pe.wait_ge(ev_done, i * 2 + (b + 1))
                    for k in range(KD):
                        last = nc.tensor.transpose(g.ps[:, 2 * b + k // 4, (k % 4) * P:(k % 4 + 1) * P], xs[:, b, k * P:(k + 1) * P], g.ident)
                    last.then_inc(tr_done, 1)


def project(nc, g, name, K, groups, w_src, nb, wbufs, evac, early=(), then=None, early_sem=0):
    early_by = [(b + early_sem, g.n_early[b + early_sem]) for b in early]
    G = len(groups)
    NB = 8
    assert G % 2 == 0 and (nb == 1 or (nb % 2 == 0 and G % NB == 0))
    pairs = nb // 2

    with stage(nc, name, "w0", "w1", "mm", "ev0", "ev1") as (block, w0, w1, mm, ev0, ev1):
        landed, emptied = (w0, w1), (ev0, ev1)

        def blocks(eng, body):
            if nb == 1:
                body(0, 0, 0)
            else:
                with eng.Fori(0, pairs) as i:
                    for b in range(2):
                        body(i * 2 + b, b, i)

        @block.sync
        def _(sp):
            for b in range(min(nb, 2)):
                if b in early:
                    credit(sp, landed[b], 16)
                else:
                    sp.dma_start(wbufs[b], w_src(b)).then_inc(landed[b], 16)
            if then is not None:
                sp.wait_ge(mm, G)
                sp.dma_start(*then).then_inc(g.early[0], 16)
            if pairs > 1:
                with sp.Fori(1, pairs) as i:
                    for b in range(2):
                        sp.wait_ge(mm, i * (2 * G) + (b - 1) * G)
                        sp.dma_start(wbufs[b], w_src(i * 2 + b)).then_inc(landed[b], 16)

        @block.tensor
        def _(pe):
            for b, n in early_by:
                pe.wait_ge(g.early[b], n)

            def body(n, b, i):
                pe.wait_ge(landed[b], i * 16 + 16)
                for j in range(G):
                    pe.wait_ge(emptied[j % 2], n * (G // 2) + (j // 2 + 1))
                    for k in range(K):
                        lhsT, rhs, out = groups[j](wbufs[b], k, g.ps[:, j % NB, :])
                        last = nc.tensor.matmul(out, lhsT, rhs, start=(k == 0), stop=(k == K - 1))
                    last.then_inc(mm, 1)
            blocks(pe, body)

        def reader(e, eng):
            credit(eng, emptied[e], NB // 2)

            def body(n, b, i):
                for j in range(e, G, 2):
                    eng.wait_ge(mm, n * G + (j + 1))
                    evac(e, n, j, g.ps[:, j % NB, :]).then_inc(emptied[e], 1)
            blocks(eng, body)

        @block.vector
        def _(dve):
            reader(0, dve)

        @block.scalar
        def _(act):
            reader(1, act)
    if then is not None:
        g.n_early[0] += 16


def start_loads(nc, g, *loads):
    with nc.Block() as block:
        @block.sync
        def _(sp):
            for b, to, of in loads:
                sp.dma_start(to, of).then_inc(g.early[b], 16)
                g.n_early[b] += 16


def by_token(xt, t, ncols):
    return lambda w, k, bank: (xt[:, k, t * P:(t + 1) * P], w[:, k, :], bank[:, 0:ncols])


def by_feature(xt, f, t0, nt):
    return lambda w, k, bank: (w[:, k, f * P:(f + 1) * P], xt[:, k, t0:t0 + nt], bank[:, 0:nt])


def copy(nc, e, out, in_):
    if e == 0:
        return nc.vector.tensor_copy(out, in_)
    return nc.scalar.activation(out, in_, ACT.Copy)


def blocks_of(w, c0, width):
    v = w.rearrange("(k p) n -> p k n", p=P)
    return lambda n: v[:, :, ds(c0 + n * width, width)] if not isinstance(n, int) else v[:, :, c0 + n * width:c0 + (n + 1) * width]


def load_stage(nc, g, I):
    loads = [
        (g.ident, I["ident"]), (g.tri, I["before"]),
        (g.x[:, :, :], I["x"].rearrange("a (t p) d -> p (a t) d", p=P)),
        (g.ctx, I["ctx"].rearrange("a (t p) d -> p (a t) d", p=P)),
    ]
    vectors = [I["c"].rearrange("a d -> (a d)"), I["c_ctx"], I["b_mod"].rearrange("a d -> (a d)"), I["norm_g"].rearrange("a d -> (a d)"),
               I["q_lora_g"].rearrange("a d -> (a d)"), I["kv_lora_g"].rearrange("a d -> (a d)"),
               I["norm_mix_g_2"].rearrange("a d -> (a d)"), I["norm_ffn_g_2"].rearrange("a d -> (a d)"),
               I["hgrn_lb_logits_2"].rearrange("a d -> (a d)"), I["gla_b_a2_2"].rearrange("a d -> (a d)")]
    stacked = g.scratch.at(0, P)
    r = 0
    for v in vectors:
        n = v.shape[0] // P
        loads.append((stacked[r:r + n, :], v.rearrange("(k p) -> k p", p=P)))
        r += n
    assert r == VECS
    with stage(nc, "load", "in", "set", "turned", "copied") as (block, arrived, was_set, turned, copied):
        @block.sync
        def _(sp):
            for to, of in loads:
                sp.dma_start(to, of).then_inc(arrived, 16)
            sp.wait_ge(arrived, 16 * len(loads))

        @block.vector
        def _(dve):
            nc.vector.memset(g.zeros, 0.0).then_inc(was_set, 1)
            nc.vector.memset(g.eps[:, 0:1], EPS).then_inc(was_set, 1)
            nc.vector.memset(g.ones, 1.0).then_inc(was_set, 1)
            dve.wait_ge(turned, 1)
            nc.vector.tensor_copy(g.vec, g.ps[:, 0, 0:VECS]).then_inc(copied, 1)

        @block.tensor
        def _(pe):
            pe.wait_ge(arrived, 16 * len(loads))
            nc.tensor.transpose(g.ps[:, 0, 0:VECS], stacked[0:VECS, :], g.ident[0:VECS, 0:VECS]).then_inc(turned, 1)


def mod_stage(nc, g, I):
    w = I["w_mod"].rearrange("a (k p) n -> k p (a n)", p=P)
    rows2 = g.scratch.at(D, 3 * D)
    wk = [g.arena.at((8192 if k < 4 else 28672) + k % 4 * 3 * D, 3 * D) for k in range(KD)]
    with stage(nc, "mod", "silu", "in", "mm", "copied", "turned", "add", "prep", "gate") as (block, silu, arrived, mm, copied, turned, add, prep, gate):
        @block.scalar
        def _(act):
            nc.scalar.activation(g.cs.rearrange("p k j -> p j k"), g.vec[:, 0:16].rearrange("p (j k) -> p j k", j=2), ACT.Silu).then_inc(silu, 1)

        @block.sync
        def _(sp):
            for k in range(KD):
                sp.dma_start(wk[k], w[k]).then_inc(arrived, 16)

        @block.tensor
        def _(pe):
            pe.wait_ge(silu, 1)
            pe.wait_ge(arrived, 16 * KD)
            for n in range(6):
                for k in range(KD):
                    last = nc.tensor.matmul(g.ps[0:2, n, :], g.cs[:, k, :], wk[k][:, n * 512:(n + 1) * 512], start=(k == 0), stop=(k == KD - 1))
                last.then_inc(mm, 1)
            pe.wait_ge(copied, 6)
            for f in range(24):
                last = nc.tensor.transpose(g.ps[:, 6, f * 2:f * 2 + 2], rows2[0:2, f * P:(f + 1) * P], g.ident[0:2, 0:2])
            last.then_inc(turned, 1)
            pe.wait_ge(prep, 1)
            for h in range(2):
                last = nc.tensor.matmul(g.ps[:, 1 + h, :], g.ones, g.scratch.at(0, D)[:, h * 512:(h + 1) * 512], start=True, stop=True)
            last.then_inc(gate, 1)

        @block.vector
        def _(dve):
            for n in range(6):
                dve.wait_ge(mm, n + 1)
                nc.vector.tensor_copy(rows2[0:2, n * 512:(n + 1) * 512], g.ps[0:2, n, :]).then_inc(copied, 1)
            dve.wait_ge(turned, 1)
            nc.vector.tensor_tensor(g.mod, g.ps[:, 6, 0:48].rearrange("p (f j) -> p f j", j=2), g.b_mod.unsqueeze(2).broadcast_to([P, 24, 2]), ALU.add)
            dve.drain()
            for j in range(2):
                nc.vector.scalar_tensor_tensor(g.a1[:, j, :], g.mod[:, 8:16, j], 1.0, g.norm_g, ALU.add, ALU.mult)
                nc.vector.tensor_copy(g.b1[:, j, :], g.mod[:, 0:8, j])
            nc.vector.tensor_tensor(g.scratch.at(0, 8, P), g.ident.unsqueeze(1).broadcast_to([P, 8, P]),
                                    g.mod[:, 16:24, 0].unsqueeze(2).broadcast_to([P, 8, P]), ALU.mult).then_inc(prep, 1)
            dve.wait_ge(gate, 1)
            nc.vector.tensor_copy(g.gate_row, g.ps[:, 1:3, :].rearrange("p a n -> p (a n)")).then_inc(add, 1)


def in_proj_stages(nc, g, I):
    w = I["w_in"].rearrange("a k n -> (a k) n")
    o_ga, o_pin, o_gp = LR, LR + 512, LR + 1024

    project(nc, g, "lr", KD, [by_token(g.ht, t, LR) for t in range(NK)], blocks_of(w, 0, LR), 1, [g.w[0][:, :, 0:LR]],
            lambda e, n, j, bank: copy(nc, e, g.lr[:, j, :], bank[:, 0:LR]), early=(0,))

    for name, off, c, b, following in (("ga", o_ga, 0, 1, o_gp), ("gp", o_gp, 512, 0, o_pin)):
        start_loads(nc, g, (1 - b, g.w[1 - b], blocks_of(w, following, 512)(0)))
        project_scalar(nc, g, name, KD, [by_token(g.ht, t, 512) for t in range(NT)], blocks_of(w, off, 512), g.w[b],
                       lambda e, n, j, bank: nc.scalar.activation(g.br[:, j, c:c + 512], bank, ACT.Silu), early=b)
    project(nc, g, "pin", KD, [by_feature(g.ht, f, h * 512, 512) for f in range(4) for h in range(2)], blocks_of(w, o_pin, 512), 1, [g.w[1]],
            lambda e, n, j, bank: copy(nc, e, g.pt[:, j // 2, PAD // 2 + (j % 2) * 512:PAD // 2 + (j % 2 + 1) * 512], bank), early=(0,), early_sem=1)


def pool_stage(nc, g, I):
    L = T + PAD
    s2, s4 = g.scratch.at(0, L), g.scratch.at(L, L)
    pooled = g.scratch.at(2 * L, T)
    inv = g.scratch.at(2 * L + T, T)
    wp = g.w[0][:, 0, 0:4 * P].rearrange("p (g n) -> p g n", g=4)
    pscale = g.w[0][:, 1, :]
    with stage(nc, "pool", "in", "inv", "pooled", "y", "out", "zero", "sem") as (block, arrived, inv_in, ready, y_done, out_done, zero, mult_done):
        @block.sync
        def _(sp):
            sp.dma_start(wp, I["w_pool"].rearrange("a g c n -> c (a g) n")).then_inc(arrived, 16)
            sp.dma_start(pscale, rows(I["pool_scale"].rearrange("a n -> (a n)"))).then_inc(arrived, 16)
            for gi in range(4):
                if gi:
                    sp.wait_ge(ready, gi)
                sp.dma_start(inv, rows(I["inv_count"][gi])).then_inc(inv_in, 16)

        @block.vector
        def _(dve):
            nc.vector.memset(g.pt[:, :, 0:PAD // 2], 0.0)
            nc.vector.memset(g.pt[:, :, PAD // 2 + T:T + PAD], 0.0)
            dve.drain()
            for gi, w in enumerate(WINDOWS):
                u = g.pt[:, gi, :]
                cur, n, bufs = u, 1, (s2, s4)
                step = 0
                while n < w:
                    to = bufs[step % 2]
                    nc.vector.tensor_tensor(to[:, 0:L - 2 * n + 1], cur[:, 0:L - 2 * n + 1], cur[:, n:L - n + 1], ALU.add)
                    dve.drain()
                    cur, n, step = to, 2 * n, step + 1
                first = PAD // 2 - w // 2
                dve.wait_ge(inv_in, 16 * (gi + 1))
                if gi:
                    dve.wait_ge(y_done, gi)
                nc.vector.tensor_tensor(pooled, cur[:, first:first + T], inv, ALU.mult)
                dve.drain()
                nc.vector.tensor_tensor(pooled, pooled, u[:, PAD // 2:PAD // 2 + T], ALU.subtract).then_inc(ready, 1)
            dve.wait_ge(y_done, 4)
            dve.wait_ge(arrived, 32)
            for t in range(NT):
                nc.vector.tensor_tensor(g.br[:, t, 512:1024], g.br[:, t, 512:1024], g.ps[:, t, :], ALU.mult)
            dve.drain()
            for t in range(NT):
                nc.vector.tensor_tensor(g.br[:, t, 512:1024], g.br[:, t, 512:1024], pscale, ALU.mult).then_inc(out_done, 1)

        @block.tensor
        def _(pe):
            pe.wait_ge(arrived, 32)
            for gi in range(4):
                pe.wait_ge(ready, gi + 1)
                for t in range(NT):
                    last = nc.tensor.matmul(g.ps[:, t, gi * P:(gi + 1) * P], pooled[:, t * P:(t + 1) * P], wp[:, gi, :], start=True, stop=True)
                last.then_inc(y_done, 1)


def lora_norm_stage(nc, g):
    ss = g.small.at(0, 2, NK)
    sq = g.small.at(2 * NK, 2, NK)
    rs = g.small.at(4 * NK, 2, NK)
    junk = g.scratch.at(0, 512)
    with stage(nc, "lora", "sq", "root", "rstd", "tr", "ev", "kr") as (block, squares, root, rstd, tr_done, ev_done, kr):
        @block.scalar
        def _(act):
            for t in range(NK):
                nc.scalar.activation(junk[:, 0:LORA_Q], g.lr[:, t, 0:LORA_Q], ACT.Square, scale=LORA_Q ** -0.5, accum_out=ss[:, 0, t:t + 1])
                nc.scalar.activation(junk[:, 256:256 + LORA_KV], g.lr[:, t, LORA_Q:LORA_Q + LORA_KV], ACT.Square, scale=LORA_KV ** -0.5, accum_out=ss[:, 1, t:t + 1])
                act.drain()
            nc.scalar.activation(sq, ss, ACT.Sqrt, bias=g.eps[:, 0:1]).then_inc(root, 1)

        @block.vector
        def _(dve):
            dve.wait_ge(root, 1)
            nc.vector.reciprocal(rs, sq)
            dve.drain()
            for a, (c0, n) in enumerate(((0, LORA_Q), (LORA_Q, LORA_KV))):
                last = nc.vector.tensor_tensor(g.lr[:, :, c0:c0 + n], g.lr[:, :, c0:c0 + n], rs[:, a, :].unsqueeze(2).broadcast_to([P, NK, n]), ALU.mult)
            last.then_inc(rstd, 1)
            nc.vector.tensor_copy(g.krt, g.lr[:, :, LORA_Q + LORA_KV:LR]).then_inc(kr, 1)
            for t in range(NK):
                dve.wait_ge(tr_done, t + 1)
                bank = g.ps[:, t % 4, 0:3 * P].rearrange("p (k t) -> p k t", k=3)
                if t < NT:
                    nc.vector.tensor_tensor(g.cqt[:, :, t * P:(t + 1) * P], bank[:, 0:2, :], g.lora_g[:, 0:2].unsqueeze(2).broadcast_to([P, 2, P]), ALU.mult)
                nc.vector.tensor_scalar(g.ckvt[:, t * P:(t + 1) * P], bank[:, 2, :], g.lora_g[:, 2:3], None, ALU.mult).then_inc(ev_done, 1)

        @block.tensor
        def _(pe):
            pe.wait_ge(rstd, 1)
            for t in range(NK):
                if t >= 4:
                    pe.wait_ge(ev_done, t - 3)
                for k in range(3):
                    last = nc.tensor.transpose(g.ps[:, t % 4, k * P:(k + 1) * P], g.lr[:, t, k * P:(k + 1) * P], g.ident)
                last.then_inc(tr_done, 1)


def head_stage(nc, g, I, name, n_tiles, K, width, lat, w_dram, out_nope, out_rope, norm_row, is_key):
    wb = g.w_small.at(0, K, width)
    half = width // 2
    SC = g.scratch
    vals_of = [SC.at(0, HEADS, QK), SC.at(2048, HEADS, QK)]
    junk = SC.at(768, HEADS, QK)
    swp = SC.at(1536, HEADS, ROPE)
    rop = SC.at(1792, HEADS, ROPE)

    def place(out, t):
        return out[:, :, t * P:(t + 1) * P] if is_key else out.rearrange("p h (q s) -> p s h q", s=NT)[:, t, :, :]

    ss_of, sq_of, rs_of = ([g.small.at(8 * i + 32 * b, HEADS) for b in range(2)] for i in range(3))
    with stage(nc, name, "in", "mm", "root", "vals", "tr", "ev", "evr", "free") as (block, arrived, mm, root, ready, tr_done, ev_done, evr, free):
        @block.sync
        def _(sp):
            sp.dma_start(wb, w_dram.rearrange("a (k p) n -> p (a k) n", p=P)).then_inc(arrived, 16)
            sp.dma_start(g.norm_row, rows(norm_row.rearrange("a n -> (a n)"))).then_inc(arrived, 16)

        @block.tensor
        def _(pe):
            def products(t):
                if t >= 2:
                    pe.wait_ge(free, t - 1)
                for h in range(2):
                    for k in range(K):
                        last = nc.tensor.matmul(g.ps[:, 2 * (t % 2) + h, 0:half], lat(k, t), wb[:, k, h * half:(h + 1) * half], start=(k == 0), stop=(k == K - 1))
                last.then_inc(mm, 1)

            pe.wait_ge(arrived, 32)
            products(0)
            for t in range(n_tiles):
                if t + 1 < n_tiles:
                    products(t + 1)
                pe.wait_ge(ready, t + 1)
                if t:
                    pe.wait_ge(ev_done, t)
                    pe.wait_ge(evr, t)
                for h in range(HEADS):
                    nc.tensor.transpose(g.ps[:, 4, h * P:(h + 1) * P], vals_of[t % 2][:, h, 0:NOPE], g.ident)
                for h in range(2):
                    last = nc.tensor.transpose(g.ps[:, 5, h * P:(h + 1) * P], rop.rearrange("p h r -> p (h r)")[:, h * P:(h + 1) * P], g.ident)
                last.then_inc(tr_done, 1)

        @block.vector
        def _(dve):
            dve.wait_ge(arrived, 32)
            for t in range(n_tiles):
                vals, sq, rs = vals_of[t % 2], sq_of[t % 2], rs_of[t % 2]
                dve.wait_ge(root, t + 1)
                nc.vector.reciprocal(rs, sq)
                dve.drain()
                nc.vector.tensor_tensor(vals, vals, rs.unsqueeze(2).broadcast_to([P, HEADS, QK]), ALU.mult)
                dve.drain()
                nc.vector.tensor_tensor(vals, vals, g.norm_row.unsqueeze(1).broadcast_to([P, HEADS, QK]), ALU.mult)
                dve.drain()
                if t:
                    dve.wait_ge(tr_done, t)
                if t < NT:
                    r = vals[:, :, NOPE:QK]
                    r5 = r.rearrange("p h (x s f) -> p h x s f", x=2, s=2)
                    s5 = swp.rearrange("p h (x s f) -> p h x s f", x=2, s=2)
                    cos = g.axial[:, 0, t, :].unsqueeze(1).broadcast_to([P, HEADS, ROPE])
                    sin = g.axial[:, 1, t, :].unsqueeze(1).broadcast_to([P, HEADS, ROPE])
                    for x in range(2):
                        for s in range(2):
                            nc.vector.tensor_copy(s5[:, :, x, s, :], r5[:, :, x, 1 - s, :])
                    nc.vector.tensor_tensor(rop, r, cos, ALU.mult)
                    dve.drain()
                    nc.vector.tensor_tensor(swp, swp, sin, ALU.mult)
                    dve.drain()
                    nc.vector.tensor_tensor(rop, rop, swp, ALU.add).then_inc(ready, 1)
                else:
                    nc.vector.tensor_copy(rop, vals[:, :, NOPE:QK]).then_inc(ready, 1)
                dve.wait_ge(tr_done, t + 1)
                nc.vector.tensor_copy(place(out_rope, t), g.ps[:, 5, 0:2 * P].rearrange("p (h t) -> p h t", h=2)).then_inc(evr, 1)

        @block.scalar
        def _(act):
            def head(t):
                vals, ss, sq = vals_of[t % 2], ss_of[t % 2], sq_of[t % 2]
                ps = g.ps[:, 2 * (t % 2):2 * (t % 2) + 2, 0:half].rearrange("p a (h n) -> p a h n", h=2)
                v4 = vals.rearrange("p (a h) n -> p a h n", a=2)
                act.wait_ge(mm, t + 1)
                if t >= 2:
                    act.wait_ge(tr_done, t - 1)
                if is_key:
                    for a in range(2):
                        nc.scalar.activation(v4[:, a, :, 0:NOPE], ps[:, a, :, 0:NOPE], ACT.Copy)
                    nc.scalar.activation(vals[:, :, NOPE:QK], g.krt[:, t, :].unsqueeze(1).broadcast_to([P, HEADS, ROPE]), ACT.Copy)
                    for a in range(2):
                        last = nc.scalar.activation(g.v[:, t, a * 256:(a + 1) * 256].rearrange("p (h n) -> p h n", h=2), ps[:, a, :, NOPE:NOPE + P], ACT.Copy)
                else:
                    for a in range(2):
                        last = nc.scalar.activation(v4[:, a, :, :], ps[:, a, :, :], ACT.Copy)
                last.then_inc(free, 1)
                act.drain()
                for h in range(HEADS):
                    nc.scalar.activation(junk[:, h, :], vals[:, h, :], ACT.Square, accum_out=ss[:, h:h + 1])
                act.drain()
                nc.scalar.activation(sq, ss, ACT.Sqrt, scale=1.0 / QK, bias=g.eps[:, 0:1]).then_inc(root, 1)

            head(0)
            for t in range(n_tiles):
                if t + 1 < n_tiles:
                    head(t + 1)
                act.wait_ge(tr_done, t + 1)
                nc.scalar.activation(place(out_nope, t), g.ps[:, 4, :].rearrange("p (h t) -> p h t", h=HEADS), ACT.Copy).then_inc(ev_done, 1)


def attention_stage(nc, g):
    scale = QK ** -0.5
    units = [(h, t) for h in range(HEADS) for t in range(NT)]
    N = len(units)
    pieces = [(0, 4), (4, 8), (8, 10)]
    mx, nm, sm, ri = (g.small.at(4 * i, 2) for i in range(4))
    with stage(nc, "attn", "sc", "max", "neg", "exp", "tr", "ev", "pv", "rec", "o") as (block, sc, maxed, neg, exped, tr_done, ev_done, pv, rec, o_done):
        @block.sync
        def _(sp):
            sp.dma_start(g.y_dram.rearrange("(p a) (b c) -> p (a b) c", p=P, c=ZERO_W), g.zeros.unsqueeze(1).broadcast_to([P, SLOTS // P * D // ZERO_W, ZERO_W])).then_inc(g.y_cleared, 16)

        @block.tensor
        def _(pe):
            def scores(u):
                h, t = units[u]
                if u >= 2:
                    pe.wait_ge(exped, u - 1)
                r0 = 64 * (h % 2)
                for i, (k0, n) in enumerate(((0, 512), (512, 512), (1024, 256))):
                    bank = g.ps[:, 3 * (u % 2) + i, 0:n]
                    nc.tensor.matmul(bank, g.qt[:, h, t * P:(t + 1) * P], g.kt[:, h, k0:k0 + n], start=True, stop=False)
                    last = nc.tensor.matmul(bank, g.qr[r0:r0 + 64, h // 2, t * P:(t + 1) * P], g.kr[r0:r0 + 64, h // 2, k0:k0 + n], start=False, stop=True)
                last.then_inc(sc, 1)

            def transposes(u, i):
                a, b = pieces[i]
                n = 3 * u + i
                if n:
                    pe.wait_ge(ev_done, n)
                for k in range(a, b):
                    last = nc.tensor.transpose(g.ps[:, 6, (k - a) * P:(k - a + 1) * P], g.p[:, u % 2, k * P:(k + 1) * P], g.ident)
                last.then_inc(tr_done, 1)

            def values(u, i):
                h, _ = units[u]
                a, b = pieces[i]
                pe.wait_ge(ev_done, 3 * u + i + 1)
                if i == 0 and u:
                    pe.wait_ge(o_done, u)
                for k in range(a, b):
                    last = nc.tensor.matmul(g.ps[:, 7, 0:P], g.ptb[:, k * P:(k + 1) * P], g.v[:, k, h * P:(h + 1) * P], start=(k == 0), stop=(k == NK - 1))
                if i == 2:
                    last.then_inc(pv, 1)

            scores(0)
            for u in range(N):
                if u + 1 < N:
                    scores(u + 1)
                pe.wait_ge(exped, u + 1)
                for i in range(3):
                    transposes(u, i)
                    if i:
                        values(u, i - 1)
                values(u, 2)

        @block.vector
        def _(dve):
            def head(u):
                b = u % 2
                dve.wait_ge(sc, u + 1)
                if u >= 2:
                    dve.wait_ge(exped, u - 1)
                nc.vector.tensor_reduce(mx[:, b:b + 1], g.ps[:, 3 * b:3 * b + 3, :].rearrange("p a n -> p (a n)")[:, 0:KEYS], AX.X, ALU.max)
                dve.drain()
                nc.vector.tensor_scalar(nm[:, b:b + 1], mx[:, b:b + 1], -scale, None, ALU.mult).then_inc(neg, 1)

            head(0)
            for u in range(N):
                if u + 1 < N:
                    head(u + 1)
                h, t = units[u]
                b = u % 2
                for i, (a0, a1) in enumerate(pieces):
                    dve.wait_ge(tr_done, 3 * u + i + 1)
                    if u:
                        dve.wait_ge(pv, u)
                    nc.vector.tensor_copy(g.ptb[:, a0 * P:a1 * P], g.ps[:, 6, 0:(a1 - a0) * P]).then_inc(ev_done, 1)
                nc.vector.reciprocal(ri[:, b:b + 1], sm[:, b:b + 1])
                dve.wait_ge(pv, u + 1)
                dve.drain()
                o = g.br[:, t, h * P:(h + 1) * P]
                nc.vector.scalar_tensor_tensor(o, g.ps[:, 7, 0:P], ri[:, b:b + 1], o, ALU.mult, ALU.mult).then_inc(o_done, 1)

        @block.scalar
        def _(act):
            for u in range(N):
                b = u % 2
                act.wait_ge(neg, u + 1)
                if u >= 2:
                    act.wait_ge(o_done, u - 1)
                nc.scalar.activation(g.p[:, b, :], g.ps[:, 3 * b:3 * b + 3, :].rearrange("p a n -> p (a n)")[:, 0:KEYS], ACT.Exp,
                                     bias=nm[:, b:b + 1], scale=scale, accum_out=sm[:, b:b + 1]).then_inc(exped, 1)


def transpose_stage(nc, g, name, src, dst, nk=KD):
    with stage(nc, name, "tr", "ev") as (block, tr_done, ev_done):
        @block.tensor
        def _(pe):
            for t in range(NT):
                b = t % 4
                if t >= 4:
                    pe.wait_ge(ev_done, t - 3)
                for k in range(nk):
                    last = nc.tensor.transpose(g.ps[:, 2 * b + k // 4, (k % 4) * P:(k % 4 + 1) * P], src[:, t, k * P:(k + 1) * P], g.ident)
                last.then_inc(tr_done, 1)

        @block.vector
        def _(dve):
            for t in range(NT):
                b = t % 4
                dve.wait_ge(tr_done, t + 1)
                nc.vector.tensor_copy(dst[:, :, t * P:(t + 1) * P], g.ps[:, 2 * b:2 * b + nk // 4, :].rearrange("p a (k t) -> p (a k) t", t=P)).then_inc(ev_done, 1)


def out_proj(nc, g, name, xt, w, gate=None, early=(), x_after=None):
    tmp = g.scratch.at(0, 512)

    def evac(e, n, j, bank):
        x = g.x[:, j, ds(n * 512, 512)] if not isinstance(n, int) else g.x[:, j, n * 512:(n + 1) * 512]
        if gate is None:
            return nc.vector.tensor_tensor(x, x, bank, ALU.add)
        nc.vector.drain()
        nc.vector.tensor_tensor(tmp, bank, gate[:, ds(n * 512, 512)], ALU.mult)
        nc.vector.drain()
        return nc.vector.tensor_tensor(x, x, tmp, ALU.add)

    project_one_reader(nc, g, name, KD, [by_token(xt, t, 512) for t in range(NT)], blocks_of(w, 0, 512), 2, g.w, evac, early, x_after)


def project_one_reader(nc, g, name, K, groups, w_src, nb, wbufs, evac, early=(), write_after=None):
    G, NB = len(groups), 8
    assert nb % 2 == 0 and G % NB == 0
    early_by = [(b, g.n_early[b]) for b in early]
    with stage(nc, name, "w0", "w1", "mm", "ev") as (block, w0, w1, mm, ev):
        landed = (w0, w1)

        @block.sync
        def _(sp):
            for b in range(2):
                if b in early:
                    credit(sp, landed[b], 16)
                else:
                    sp.dma_start(wbufs[b], w_src(b)).then_inc(landed[b], 16)
            if nb > 2:
                with sp.Fori(1, nb // 2) as i:
                    for b in range(2):
                        sp.wait_ge(mm, i * (2 * G) + (b - 1) * G)
                        sp.dma_start(wbufs[b], w_src(i * 2 + b)).then_inc(landed[b], 16)

        @block.tensor
        def _(pe):
            for b, n in early_by:
                pe.wait_ge(g.early[b], n)
            with pe.Fori(0, nb // 2) as i:
                for b in range(2):
                    pe.wait_ge(landed[b], i * 16 + 16)
                    for j in range(G):
                        pe.wait_ge(ev, i * (2 * G) + (b * G + j + 1))
                        for k in range(K):
                            lhsT, rhs, out = groups[j](wbufs[b], k, g.ps[:, j % NB, :])
                            last = nc.tensor.matmul(out, lhsT, rhs, start=(k == 0), stop=(k == K - 1))
                        last.then_inc(mm, 1)

        @block.vector
        def _(dve):
            credit(dve, ev, NB)
            if write_after is not None:
                dve.wait_ge(*write_after)
            with dve.Fori(0, nb // 2) as i:
                for b in range(2):
                    for j in range(G):
                        dve.wait_ge(mm, i * (2 * G) + (b * G + j + 1))
                        evac(0, i * 2 + b, j, g.ps[:, j % NB, :]).then_inc(ev, 1)



def pieces_of_two_pi(bits=7, n=7):
    out, rest = [], TWO_PI
    for _ in range(n):
        e = math.floor(math.log2(rest)) - bits + 1
        out.append(math.floor(rest / 2.0 ** e) * 2.0 ** e)
        rest -= out[-1]
    return out


def rotary_table_stage(nc, g, I):
    pos_i = g.scratch.at(0, P).bitcast(I32)
    pos_r, freq, ang = g.scratch.at(P, P), g.scratch.at(2 * P, 64), g.scratch.at(512, NT, 64)
    n, rc = g.scratch.at(1024, NT, 64), g.scratch.at(1536, NT, 64)
    posc = g.small.at(0, NT)
    MAGIC = 1.5 * 2 ** 23
    LIMIT = float(np.nextafter(np.float32(math.pi), np.float32(0)))
    with stage(nc, "rot", "in", "float", "turned", "angles", "out") as (block, arrived, floated, turned, angles, done):
        @block.sync
        def _(sp):
            sp.dma_start(pos_i[0:NT, :], I["positions_2"].rearrange("a (t p) -> (a t) p", p=P)).then_inc(arrived, 16)
            sp.dma_start(freq, rows(I["inv_freq"])).then_inc(arrived, 16)

        @block.tensor
        def _(pe):
            pe.wait_ge(floated, 1)
            nc.tensor.transpose(g.ps[:, 0, 0:NT], pos_r[0:NT, :], g.ident[0:NT, 0:NT]).then_inc(turned, 1)

        @block.vector
        def _(dve):
            v = nc.vector
            dve.wait_ge(arrived, 32)
            v.tensor_copy(pos_r[0:NT, :], pos_i[0:NT, :]).then_inc(floated, 1)
            dve.wait_ge(turned, 1)
            v.tensor_copy(posc, g.ps[:, 0, 0:NT])
            dve.drain()
            v.tensor_tensor(ang, posc.unsqueeze(2).broadcast_to([P, NT, 64]), freq.unsqueeze(1).broadcast_to([P, NT, 64]), ALU.mult)
            dve.drain()
            v.tensor_scalar(n, ang, 1.0 / TWO_PI, MAGIC, ALU.mult, ALU.add)
            dve.drain()
            v.tensor_scalar(n, n, -MAGIC, None, ALU.add)
            for c in pieces_of_two_pi():
                dve.drain()
                v.scalar_tensor_tensor(ang, n, -c, ang, ALU.mult, ALU.add)
            dve.drain()
            v.tensor_scalar(ang, ang, -LIMIT, LIMIT, ALU.max, ALU.min)
            dve.drain()
            v.tensor_scalar(n, ang, math.pi / 2, -TWO_PI, ALU.is_gt, ALU.mult)
            dve.drain()
            v.scalar_tensor_tensor(rc, ang, math.pi / 2, n, ALU.add, ALU.add)
            dve.drain()
            v.tensor_scalar(rc, rc, -LIMIT, LIMIT, ALU.max, ALU.min).then_inc(angles, 1)

        @block.scalar
        def _(act):
            act.wait_ge(angles, 1)
            nc.scalar.activation(g.axial[:, 0, :, :], rc, ACT.Sin)
            nc.scalar.activation(g.axial[:, 1, :, :], ang, ACT.Sin).then_inc(done, 1)


def rotate_stage(nc, g, name, src, tmp):
    a, b, c, d = (tmp.at(i * 2048, NT, HEADS, 64) for i in range(4))
    x = src.rearrange("p t (h s f) -> p t h s f", h=HEADS, s=2)
    with stage(nc, name, "ab", "cd", "done") as (block, ab, cd, done):
        def tables(i, t):
            return g.axial[:, i, t, :].unsqueeze(1).broadcast_to([P, HEADS, 64])

        @block.vector
        def _(dve):
            for t in range(NT):
                nc.vector.tensor_tensor(a[:, t], x[:, t, :, 0, :], tables(0, t), ALU.mult)
                nc.vector.tensor_tensor(b[:, t], x[:, t, :, 1, :], tables(1, t), ALU.mult)
            dve.drain().then_inc(ab, 1)
            dve.wait_ge(cd, 1)
            nc.vector.tensor_tensor(x[:, :, :, 0, :].rearrange("p t h f -> p (t h) f"), a.rearrange("p t h f -> p (t h) f"), b.rearrange("p t h f -> p (t h) f"), ALU.subtract).then_inc(done, 1)
            nc.vector.tensor_tensor(x[:, :, :, 1, :].rearrange("p t h f -> p (t h) f"), c.rearrange("p t h f -> p (t h) f"), d.rearrange("p t h f -> p (t h) f"), ALU.add).then_inc(done, 1)

        @block.gpsimd
        def _(pool):
            for t in range(NT):
                nc.gpsimd.tensor_tensor(c[:, t], x[:, t, :, 1, :], tables(0, t), ALU.mult)
                nc.gpsimd.tensor_tensor(d[:, t], x[:, t, :, 0, :], tables(1, t), ALU.mult)
            pool.drain().then_inc(cd, 1)


def retention_stage(nc, g, I, qt, kt, k_tok, v):
    S = g.scratch
    mask, qdec, cdec = S.at(0, HEADS, P), S.at(512, HEADS, P), S.at(1024, HEADS * P)
    kc, qd, st, kd, state = (S.at(1536 + 512 * i, HEADS, P) for i in range(5))
    kdec = g.small.at(0, HEADS)
    with stage(nc, "ret", "in", "kq", "kd", "st", "stm", "sp", "su", "od", "ov") as (block, arrived, kq, kd_ready, st_done, masked, sp_done, updated, o_done, stored):
        @block.sync
        def _(sp):
            sp.dma_start(mask, I["ret_mask"]).then_inc(arrived, 16)
            sp.dma_start(qdec.rearrange("p h t -> p (h t)"), rows(I["ret_q"].rearrange("h t -> (h t)"))).then_inc(arrived, 16)
            sp.dma_start(cdec, rows(I["ret_chunk"])).then_inc(arrived, 16)
            sp.dma_start(kdec, I["ret_k"]).then_inc(arrived, 16)

        @block.gpsimd
        def _(pool):
            credit(pool, sp_done, 1)
            pool.wait_ge(arrived, 64)
            with pool.Fori(0, NT) as c:
                pool.wait_ge(o_done, c + 1)
                nc.gpsimd.tensor_copy(kc, kt[:, :, ds(c * P, P)])
                nc.gpsimd.tensor_tensor(qd, qt[:, :, ds(c * P, P)], qdec, ALU.mult).then_inc(kq, 1)
                pool.wait_ge(sp_done, c + 1)
                nc.gpsimd.tensor_tensor(kd, k_tok[:, ds(c, 1), :].rearrange("p a (h d) -> p (a h) d", h=HEADS), kdec.unsqueeze(2).broadcast_to([P, HEADS, P]), ALU.mult).then_inc(kd_ready, 1)

        @block.tensor
        def _(pe):
            credit(pe, o_done, 1)
            with pe.Fori(0, NT) as c:
                pe.wait_ge(kq, c + 1)
                pe.wait_ge(masked, c + 1)
                for h in range(HEADS):
                    last = nc.tensor.matmul(g.ps[:, 0, h * P:(h + 1) * P], kc[:, h, :], qt[:, h:h + 1, ds(c * P, P)].rearrange("p a t -> p (a t)"), start=True, stop=True)
                last.then_inc(st_done, 1)
                pe.wait_ge(kd_ready, c + 1)
                pe.wait_ge(updated, c + 1)
                for h in range(HEADS):
                    last = nc.tensor.matmul(g.ps[:, 1, h * P:(h + 1) * P], kd[:, h, :], v[:, ds(c, 1), h * P:(h + 1) * P].rearrange("p a n -> p (a n)"), start=True, stop=True)
                last.then_inc(sp_done, 1)
                pe.wait_ge(masked, c + 2)
                pe.wait_ge(stored, c + 1)
                for h in range(HEADS):
                    nc.tensor.matmul(g.ps[:, 2, h * P:(h + 1) * P], st[:, h, :], v[:, ds(c, 1), h * P:(h + 1) * P].rearrange("p a n -> p (a n)"), start=True, stop=False)
                    last = nc.tensor.matmul(g.ps[:, 2, h * P:(h + 1) * P], qd[:, h, :], state[:, h, :], start=False, stop=True)
                last.then_inc(o_done, 1)

        @block.vector
        def _(dve):
            credit(dve, masked, 1)
            nc.vector.memset(state, 0.0).then_inc(updated, 1)
            dve.wait_ge(arrived, 64)
            with dve.Fori(0, NT) as c:
                dve.wait_ge(st_done, c + 1)
                dve.wait_ge(o_done, c + 1)
                nc.vector.tensor_tensor(st, g.ps[:, 0, :].rearrange("p (h t) -> p h t", h=HEADS), mask, ALU.mult).then_inc(masked, 1)
                dve.wait_ge(sp_done, c + 2)
                dve.wait_ge(o_done, c + 2)
                flat = state.rearrange("p h d -> p (h d)")
                nc.vector.tensor_tensor(flat, flat, cdec, ALU.mult)
                dve.drain()
                nc.vector.tensor_tensor(flat, flat, g.ps[:, 1, :], ALU.add).then_inc(updated, 1)

        @block.scalar
        def _(act):
            credit(act, stored, 1)
            with act.Fori(0, NT) as c:
                act.wait_ge(o_done, c + 2)
                nc.scalar.activation(v[:, ds(c, 1), :].rearrange("p a n -> p (a n)"), g.ps[:, 2, :], ACT.Copy).then_inc(stored, 1)


def head_norm_stage(nc, g, I, name, o, heads, norm_vec, gates, tmp, gates_in=None):
    o4 = o.rearrange("p t (h d) -> p (t h) d", h=heads)
    n = NT * heads
    t4 = tmp.at(0, n, P)
    ss, sq, rs = tmp.at(n * P, n), tmp.at(n * P + n, n), tmp.at(n * P + 2 * n, n)
    row = g.norm_row[:, 0:P]
    pool_tiles = NT * 4 // heads

    def weigh(eng, t):
        g4 = gates[:, t, :].rearrange("p (h d) -> p h d", h=heads)
        return eng.tensor_tensor(g4, g4, row.unsqueeze(1).broadcast_to([P, heads, P]), ALU.mult)

    with stage(nc, name, "in", "sq", "ss", "root", "gw", "done") as (block, arrived, squared, summed, root, weighted, done):
        @block.sync
        def _(sp):
            sp.dma_start(row, rows(norm_vec)).then_inc(arrived, 16)

        @block.gpsimd
        def _(pool):
            pool.wait_ge(arrived, 16)
            if gates_in is not None:
                pool.wait_ge(*gates_in)
            for t in range(pool_tiles):
                last = weigh(nc.gpsimd, t)
            last.then_inc(weighted, 1)

        @block.scalar
        def _(act):
            nc.scalar.activation(t4, o4, ACT.Square).then_inc(squared, 1)
            act.wait_ge(summed, 1)
            nc.scalar.activation(sq, ss, ACT.Sqrt, scale=1.0 / P, bias=g.eps[:, 0:1]).then_inc(root, 1)

        @block.vector
        def _(dve):
            dve.wait_ge(squared, 1)
            nc.vector.tensor_reduce(ss, t4, AX.X, ALU.add).then_inc(summed, 1)
            dve.wait_ge(root, 1)
            nc.vector.reciprocal(rs, sq)
            dve.drain()
            nc.vector.tensor_tensor(o4, o4, rs.unsqueeze(2).broadcast_to([P, n, P]), ALU.mult)
            dve.drain()
            if pool_tiles < NT:
                dve.wait_ge(arrived, 16)
                if gates_in is not None:
                    dve.wait_ge(*gates_in)
                for t in range(pool_tiles, NT):
                    weigh(nc.vector, t)
                dve.drain()
            dve.wait_ge(weighted, 1)
            for t in range(NT):
                last = nc.vector.tensor_tensor(gates[:, t, :], gates[:, t, :], o[:, t, :], ALU.mult)
            last.then_inc(done, 1)


def gated_stage(nc, g, I, name, F, hp, qt, kt, lf, v, qscale, S):
    W = F * P
    H = F * hp
    dk = P // hp
    G, qc, kc, eq, ek, kd, state = (S.at(i * W, F, P) for i in range(7))
    base = 7 * W
    e = [S.at(base + i * W, F, P) for i in range(2)]
    ql = [S.at(base + (2 + i) * W, F, P) for i in range(2)]
    kl = [S.at(base + (4 + i) * W, F, P) for i in range(2)]
    st = S.at(base + 6 * W, H, P)
    mask = S.at(base + 6 * W + H * P, NLEV, P).bitcast(U32)
    eg = g.small.at(0, F)
    L = NLEV
    sems = ("in", "qk", "G", "e0", "diff", "e", "ql", "kl", "kg", "qg", "st", "cp", "trk", "kd", "sp", "su", "od", "ov", "zero")
    with stage(nc, name, *sems) as (block, arrived, qk, g_ready, e0, diff, exped, ql_ready, kl_ready, kg, qg, st_done, picked, trk, kd_ready, sp_done, updated, o_done, stored, zeroed):
        def halves(x, s):
            y = x.rearrange("p f (b u s) -> p (f b) u s", u=2, s=s)
            return y[:, :, 0, :], y[:, :, 1, :]

        def slot(h):
            return h % hp * F + h // hp if hp > 1 else h

        def middle(s):
            left, _ = halves(G, s)
            return left[:, :, s - 1:s].broadcast_to([P, F * (P // (2 * s)), s])

        @block.sync
        def _(sp):
            sp.dma_start(mask.rearrange("p l t -> p (l t)"), I["level_mask"].rearrange("j l i -> j (l i)")).then_inc(arrived, 16)

        @block.gpsimd
        def _(pool):
            pool.wait_ge(zeroed, 1)
            with pool.Fori(0, NT) as c:
                pool.drain()
                pool.wait_ge(st_done, c * L + 1)
                pool.wait_ge(qg, c + 1)
                pool.wait_ge(zeroed, 1)
                nc.gpsimd.tensor_tensor(qc, qt[:, :, ds(c * P, P)], g.qs.unsqueeze(1).broadcast_to([P, F, P]), ALU.mult)
                nc.gpsimd.tensor_copy(kc, kt[:, :, ds(c * P, P)]).then_inc(qk, 1)
                pool.drain()
                pool.wait_ge(e0, c + 1)
                nc.gpsimd.tensor_tensor(ek, ek, kc, ALU.mult).then_inc(kg, 1)
                for m in range(1, L):
                    pool.wait_ge(exped, c * (L - 1) + m)
                    pool.wait_ge(st_done, c * L + m)
                    el, _ = halves(e[m % 2], LEVELS[m - 1])
                    nc.gpsimd.tensor_tensor(halves(kl[m % 2], LEVELS[m - 1])[0], halves(kc, LEVELS[m - 1])[0], el, ALU.mult).then_inc(kl_ready, 1)

        @block.vector
        def _(dve):
            v_ = nc.vector
            v_.memset(state, 0.0)
            v_.memset(g.qs, qscale)
            v_.memset(st, 0.0)
            for b in range(2):
                v_.memset(ql[b], 0.0)
                v_.memset(kl[b], 0.0)
            dve.drain()
            v_.memset(eg, 0.0).then_inc(zeroed, 1)
            credit(dve, qg, 1)
            credit(dve, updated, 1)
            credit(dve, picked, 2)
            dve.wait_ge(arrived, 16)

            def differences(c, m):
                s = LEVELS[m - 1]
                gl, gr = halves(G, s)
                dl, dr = halves(e[m % 2], s)
                v_.tensor_tensor(dl, middle(s), gl, ALU.subtract)
                v_.tensor_tensor(dr, gr, middle(s), ALU.subtract).then_inc(diff, 1)

            def pick(c, m):
                dve.wait_ge(st_done, c * L + m + 2)
                dve.wait_ge(picked, c * L + m + 2)
                v_.memset(g.mark[:, 0:1], 0.0)
                bank = g.ps[:, 2 * (m % 2):2 * (m % 2) + 2, 0:H * P // 2].rearrange("p a (h i) -> p a h i", i=P)
                keep = mask[:, (m - 1) % L, :].unsqueeze(1).unsqueeze(1).broadcast_to([P, 2, H // 2, P])
                v_.copy_predicated(st.rearrange("p (a h) i -> p a h i", a=2), keep, bank).then_inc(picked, 1)

            with dve.Fori(0, NT) as c:
                dve.drain()
                dve.wait_ge(kl_ready, c * (L - 1) + 1)
                for f in range(F):
                    v_.tensor_tensor_scan(G[:, f, :], g.ones, lf[:, f:f + 1, ds(c * P, P)].rearrange("p a t -> p (a t)"), 0.0, ALU.mult, ALU.add)
                dve.drain()
                dve.wait_ge(trk, c + 1)
                v_.tensor_tensor(ek, G[:, :, P - 1:P].broadcast_to([P, F, P]), G, ALU.subtract).then_inc(g_ready, 1)
                differences(c, 1)
                dve.wait_ge(e0, c + 1)
                dve.wait_ge(qk, c + 1)
                v_.tensor_tensor(eq, eq, qc, ALU.mult).then_inc(qg, 1)
                dve.wait_ge(o_done, c + 1)
                pick(c, 0)
                for m in range(1, L):
                    if m + 1 < L:
                        if m > 1:
                            dve.drain()
                            dve.wait_ge(kl_ready, c * (L - 1) + m)
                        differences(c, m + 1)
                    dve.wait_ge(exped, c * (L - 1) + m)
                    dve.wait_ge(st_done, c * L + m)
                    v_.tensor_tensor(halves(ql[m % 2], LEVELS[m - 1])[1], halves(qc, LEVELS[m - 1])[1], halves(e[m % 2], LEVELS[m - 1])[1], ALU.mult).then_inc(ql_ready, 1)
                    if m > 1:
                        pick(c, m - 1)
                pick(c, L - 1)
                dve.wait_ge(o_done, c + 2)
                dve.wait_ge(sp_done, c + 1)
                v_.tensor_tensor(state, state, eg.unsqueeze(2).broadcast_to([P, F, P]), ALU.mult)
                dve.drain()
                if hp == 1:
                    v_.tensor_tensor(state, state, g.ps[:, 6:8, :].rearrange("p a (f n) -> p (a f) n", n=P), ALU.add).then_inc(updated, 1)
                else:
                    ps = g.ps[:, 6, :].rearrange("p (f h n) -> p f h n", f=F, h=2)
                    v_.tensor_tensor(state[0:64], state[0:64], ps[0:64, :, 0, :], ALU.add)
                    v_.tensor_tensor(state[64:128], state[64:128], ps[64:128, :, 1, :], ALU.add).then_inc(updated, 1)

        @block.scalar
        def _(act):
            credit(act, kl_ready, 1)
            credit(act, stored, 1)
            with act.Fori(0, NT) as c:
                act.wait_ge(g_ready, c + 1)
                act.wait_ge(o_done, c + 1)
                act.wait_ge(updated, c + 1)
                nc.scalar.activation(eq, G, ACT.Exp)
                nc.scalar.activation(eg, G[:, :, P - 1], ACT.Exp)
                nc.scalar.activation(ek, ek, ACT.Exp).then_inc(e0, 1)
                for m in range(1, L):
                    act.wait_ge(diff, c * (L - 1) + m)
                    nc.scalar.activation(e[m % 2], e[m % 2], ACT.Exp).then_inc(exped, 1)
                    if m == 2:
                        act.wait_ge(trk, c + 2)
                        nc.scalar.activation(kd, g.ps[:, 6:6 + (W + 511) // 512, :].rearrange("p a (f n) -> p (a f) n", n=P)[:, 0:F, :], ACT.Copy).then_inc(kd_ready, 1)
                act.wait_ge(o_done, c + 2)
                to = v[:, ds(c, 1), :].rearrange("p a (h n) -> p (a h) n", n=P)
                to = to.rearrange("p (f a) n -> p a f n", a=2) if hp == 2 else to.rearrange("p (a f) n -> p a f n", a=2)
                nc.scalar.activation(to, g.ps[:, 4:6, 0:H * P // 2].rearrange("p a (f n) -> p a f n", n=P), ACT.Copy).then_inc(stored, 1)

        @block.tensor
        def _(pe):
            credit(pe, st_done, 1)
            credit(pe, trk, 1)
            credit(pe, o_done, 1)

            def scores(c, m, k_, q_):
                pe.wait_ge(picked, c * L + (m + 1))
                for h in range(H):
                    r = dk * (h % hp)
                    f = h // hp
                    b, i = divmod(slot(h), H // 2)
                    last = nc.tensor.matmul(g.ps[:, 2 * (m % 2) + b, i * P:(i + 1) * P], k_[r:r + dk, f, :], q_[r:r + dk, f, :], start=True, stop=True)
                last.then_inc(st_done, 1)

            with pe.Fori(0, NT) as c:
                pe.wait_ge(qk, c + 1)
                scores(c, 0, kc, qc)
                pe.wait_ge(kg, c + 1)
                pe.wait_ge(updated, c + 1)
                for f in range(F):
                    last = nc.tensor.transpose(g.ps[:, 6 + f // 4, (f % 4) * P:(f % 4 + 1) * P], ek[:, f, :], g.ident)
                last.then_inc(trk, 1)
                for m in range(1, L):
                    pe.wait_ge(ql_ready, c * (L - 1) + m)
                    pe.wait_ge(kl_ready, c * (L - 1) + m + 1)
                    scores(c, m, kl[m % 2], ql[m % 2])
                    if m == 3:
                        pe.wait_ge(kd_ready, c + 1)
                        n = hp * P
                        for f in range(F):
                            out = g.ps[:, 6 + f * n // 512, f * n % 512:f * n % 512 + n]
                            last = nc.tensor.matmul(out, kd[:, f, :], v[:, ds(c, 1), f * n:(f + 1) * n].rearrange("p a n -> p (a n)"), start=True, stop=True)
                        last.then_inc(sp_done, 1)
                pe.wait_ge(picked, c * L + (L + 2))
                pe.wait_ge(qg, c + 2)
                pe.wait_ge(updated, c + 1)
                pe.wait_ge(stored, c + 1)
                for h in range(H):
                    r = dk * (h % hp)
                    b, i = divmod(slot(h), H // 2)
                    out = g.ps[:, 4 + b, i * P:(i + 1) * P]
                    nc.tensor.matmul(out, st[:, slot(h), :], v[:, ds(c, 1), h * P:(h + 1) * P].rearrange("p a n -> p (a n)"), start=True, stop=False)
                    last = nc.tensor.matmul(out, eq[r:r + dk, h // hp, :], state[r:r + dk, h // hp, :], start=False, stop=True)
                last.then_inc(o_done, 1)



def swiglu_up_stage(nc, g, name, xt, w_gate, w_up, out, n_f, tmp):
    wg, wu = blocks_of(w_gate, 0, P), blocks_of(w_up, 0, P)
    buf = [w.rearrange("p k n -> p (k n)")[:, 0:KD * 2 * P].rearrange("p (k n) -> p k n", k=KD) for w in g.w]
    with stage(nc, name, "w0", "w1", "mm", "sg", "hv") as (block, w0, w1, mm, silu, hidden):
        landed = (w0, w1)

        def load(sp, n, b):
            sp.dma_start(buf[b][:, :, 0:P], wg(n)).then_inc(landed[b], 16)
            sp.dma_start(buf[b][:, :, P:2 * P], wu(n)).then_inc(landed[b], 16)

        @block.sync
        def _(sp):
            for b in range(2):
                load(sp, b, b)
            with sp.Fori(1, n_f // 2) as i:
                for b in range(2):
                    sp.wait_ge(mm, i * 4 + (2 * b - 2))
                    load(sp, i * 2 + b, b)

        @block.tensor
        def _(pe):
            with pe.Fori(0, n_f // 2) as i:
                for b in range(2):
                    pe.wait_ge(landed[b], i * 32 + 32)
                    for h in range(2):
                        pe.wait_ge(hidden, i * 4 + (2 * b + h + 1))
                        for a in range(2):
                            for k in range(KD):
                                last = nc.tensor.matmul(g.ps[:, 4 * b + 2 * h + a, :], buf[b][:, k, a * P:(a + 1) * P], xt[:, k, h * 512:(h + 1) * 512],
                                                        start=(k == 0), stop=(k == KD - 1))
                        last.then_inc(mm, 1)

        @block.scalar
        def _(act):
            with act.Fori(0, n_f // 2) as i:
                for j in range(4):
                    act.wait_ge(mm, i * 4 + (j + 1))
                    act.wait_ge(hidden, i * 4 + (j + 1))
                    nc.scalar.activation(tmp[:, j, :], g.ps[:, 2 * j, :], ACT.Silu).then_inc(silu, 1)

        @block.vector
        def _(dve):
            credit(dve, hidden, 4)
            with dve.Fori(0, n_f // 2) as i:
                for j in range(4):
                    dve.wait_ge(silu, i * 4 + (j + 1))
                    nc.vector.tensor_tensor(out[:, ds(i * 2 + j // 2, 1), (j % 2) * 512:(j % 2 + 1) * 512].rearrange("p a n -> p (a n)"), tmp[:, j, :], g.ps[:, 2 * j + 1, :], ALU.mult).then_inc(hidden, 1)


def gla_decay_stage(nc, g, I, bat, la):
    wa = g.scratch.at(0, 2 * P)
    z, a = g.scratch.at(256, 2, T), g.scratch.at(256 + 2048, 2, T)
    with stage(nc, "decay", "in", "mm", "z", "l", "done") as (block, arrived, mm, zed, logged, done):
        @block.sync
        def _(sp):
            sp.dma_start(wa[0:16, :], I["gla_w_a2_2"].rearrange("a r n -> (a r) n")).then_inc(arrived, 16)

        @block.tensor
        def _(pe):
            pe.wait_ge(arrived, 16)
            for f in range(2):
                for h in range(2):
                    last = nc.tensor.matmul(g.ps[:, 2 * f + h, :], wa[0:16, f * P:(f + 1) * P], bat[0:16, h * 512:(h + 1) * 512], start=True, stop=True)
            last.then_inc(mm, 1)

        @block.vector
        def _(dve):
            dve.wait_ge(mm, 1)
            for f in range(2):
                last = nc.vector.tensor_scalar(z[:, f, :], g.ps[:, 2 * f:2 * f + 2, :].rearrange("p a n -> p (a n)"), g.ba2[:, f:f + 1], None, ALU.add)
            last.then_inc(zed, 1)
            dve.wait_ge(logged, 1)
            nc.vector.scalar_tensor_tensor(la, z, 0.0, a, ALU.min, ALU.subtract)
            dve.drain()
            nc.vector.tensor_scalar(la, la, 1.0 / 16, None, ALU.mult).then_inc(done, 1)

        @block.scalar
        def _(act):
            act.wait_ge(zed, 1)
            nc.scalar.activation(a, z, ACT.Abs)
            act.drain()
            nc.scalar.activation(a, a, ACT.Exp, scale=-1.0)
            act.drain()
            nc.scalar.activation(a, a, ACT.Ln, bias=1.0).then_inc(logged, 1)


def plain(nc, out, c0=0):
    return lambda e, n, j, bank: copy(nc, e, out[:, j, c0:c0 + 512], bank)


def layer_zero(nc, g, I):
    A = g.arena
    w = I["ab_w_in_2"].rearrange("a k n -> (a k) n")
    g.ht = A.at(16384, KD, T)
    o = A.at(24576, NT, D)
    R = 32768
    g.scratch = Arena_at(A, R)
    tiles = [by_token(g.ht, t, 512) for t in range(NT)]
    start_loads(nc, g, (0, g.w[0], blocks_of(w, 0, 512)(0)), (1, g.w[1], blocks_of(w, 512, 512)(0)))
    norm_stage(nc, g, "n0", g.x, NT, D, g.ht, g.mix_g[:, 0:8])
    qt, kt, k, q = A.at(R, HEADS, T), A.at(R + 4096, HEADS, T), A.at(R + 8192, NT, 512), A.at(R + 12288, NT, 512)
    rotary_table_stage(nc, g, I)
    project(nc, g, "aq", KD, tiles, blocks_of(w, 0, 512), 1, [g.w[0]], plain(nc, q), early=(0,))
    project(nc, g, "ak", KD, tiles, blocks_of(w, 512, 512), 1, [g.w[1]], plain(nc, k), early=(0,), early_sem=1)
    rotate_stage(nc, g, "rq", q, Arena_at(A, 8192))
    rotate_stage(nc, g, "rk", k, Arena_at(A, 8192))
    start_loads(nc, g, (0, g.w[0], blocks_of(w, 1024, 512)(0)), (1, g.w[1], blocks_of(w, 1536, 512)(0)))
    transpose_stage(nc, g, "qt", q, qt, 4)
    transpose_stage(nc, g, "kt", k, kt, 4)
    v = q
    project(nc, g, "av", KD, tiles, blocks_of(w, 1024, 512), 1, [g.w[0]], plain(nc, v), early=(0,))

    def gate(c0):
        def evac(e, n, j, bank):
            return nc.scalar.activation(o[:, j, c0:c0 + 512], bank, ACT.Silu)
        return evac
    project_scalar(nc, g, "ag", KD, tiles, blocks_of(w, 1536, 512), g.w[1], gate(0), early=1)
    g.scratch = Arena_at(A, 8192)
    retention_stage(nc, g, I, qt, kt, k, v)
    head_norm_stage(nc, g, I, "rn", v, 4, I["ret_norm_g_2"].rearrange("a n -> (a n)"), o[:, :, 0:512], Arena_at(A, 8192))
    bqk, la, bv = A.at(R, 4, T), A.at(R + 4096, 2, T), A.at(R + 6144, NT, 512)
    bat = A.at(R + 10240, T)
    start_loads(nc, g, (0, g.w[0], blocks_of(w, 2048, 512)(0)), (1, g.w[1], blocks_of(w, 2560, 512)(0)))
    project(nc, g, "bqk", KD, [by_feature(g.ht, f, h * 512, 512) for f in range(4) for h in range(2)], blocks_of(w, 2048, 512), 1, [g.w[0]],
            lambda e, n, j, bank: copy(nc, e, bqk[:, j // 2, (j % 2) * 512:(j % 2 + 1) * 512], bank), early=(0,))
    start_loads(nc, g, (0, g.w[0], blocks_of(w, 3072, 512)(0)))
    project(nc, g, "bv", KD, tiles, blocks_of(w, 2560, 512), 1, [g.w[1]], plain(nc, bv), early=(0,), early_sem=1)
    start_loads(nc, g, (1, g.w[1][:, :, 0:16], blocks_of(w, 3584, 16)(0)))
    project_scalar(nc, g, "bg", KD, tiles, blocks_of(w, 3072, 512), g.w[0], gate(512), early=0)
    project(nc, g, "ba", KD, [lambda w_, k_, bank, h=h: (w_[:, k_, :], g.ht[:, k_, h * 512:(h + 1) * 512], bank[0:16, :]) for h in range(2)],
            blocks_of(w, 3584, 16), 1, [g.w[1][:, :, 0:16]], lambda e, n, j, bank: copy(nc, e, bat[0:16, j * 512:(j + 1) * 512], bank[0:16, :]), early=(0,), early_sem=1)
    g.scratch = Arena_at(A, R + 11264)
    gla_decay_stage(nc, g, I, bat, la)
    gated_stage(nc, g, I, "gla", 2, 2, bqk[:, 0:2, :], bqk[:, 2:4, :], la, bv, 64 ** -0.5, Arena_at(A, 8192))
    head_norm_stage(nc, g, I, "gn", bv, 4, I["gla_norm_g_2"].rearrange("a n -> (a n)"), o[:, :, 512:1024], Arena_at(A, 8192))
    w_ab = I["ab_w_out_2"].rearrange("a k n -> (a k) n")
    start_loads(nc, g, (0, g.w[0], blocks_of(w_ab, 0, 512)(0)), (1, g.w[1], blocks_of(w_ab, 0, 512)(1)))
    transpose_stage(nc, g, "ot", o, g.ht)
    out_proj(nc, g, "abo", g.ht, w_ab, early=(0, 1))
    h = A.at(24576, FF_T, T)
    g.scratch = Arena_at(A, 24576)
    g.ht = A.at(16384, KD, T)
    norm_stage(nc, g, "n1", g.x, NT, D, g.ht, g.ffn_g[:, 0:8])
    swiglu_up_stage(nc, g, "up", g.ht, I["ffn_w_gate_2"].rearrange("a k n -> (a k) n"), I["ffn_w_up_2"].rearrange("a k n -> (a k) n"), h, FF_T, A.at(10240, 4, 512))
    wd = [A.at(8192, FF_T, 256), A.at(13824, FF_T, 256)]

    def evac(e, n, j, bank):
        x = g.x[:, j, ds(n * 256, 256)]
        return nc.vector.tensor_tensor(x, x, bank[:, 0:256], ALU.add)
    project_one_reader(nc, g, "down", FF_T, [by_token(h, t, 256) for t in range(NT)], blocks_of(I["ffn_w_down_2"].rearrange("a k n -> (a k) n"), 0, 256), 4, wd, evac)


def project_scalar(nc, g, name, K, groups, w_src, wbuf, evac, early=None):
    early_by = g.n_early[early] if early is not None else 0
    with stage(nc, name, "w", "mm", "ev") as (block, landed, mm, ev):
        @block.sync
        def _(sp):
            if early is None:
                sp.dma_start(wbuf, w_src(0)).then_inc(landed, 16)

        @block.tensor
        def _(pe):
            if early is None:
                pe.wait_ge(landed, 16)
            else:
                pe.wait_ge(g.early[early], early_by)
            for j in range(len(groups)):
                if j >= 8:
                    pe.wait_ge(ev, j - 7)
                for k in range(K):
                    lhsT, rhs, out = groups[j](wbuf, k, g.ps[:, j % 8, :])
                    last = nc.tensor.matmul(out, lhsT, rhs, start=(k == 0), stop=(k == K - 1))
                last.then_inc(mm, 1)

        @block.scalar
        def _(act):
            for j in range(len(groups)):
                act.wait_ge(mm, j + 1)
                evac(1, 0, j, g.ps[:, j % 8, :]).then_inc(ev, 1)



def lower_bound_stage(nc, g):
    d, a, l, m = (g.small.at(8 * i, 8) for i in range(4))
    with stage(nc, "lb", "d", "l", "done") as (block, made, logged, done):
        @block.vector
        def _(dve):
            nc.vector.tensor_tensor(d, g.lb[:, 0:8], g.lb[:, 8:16], ALU.subtract).then_inc(made, 1)
            dve.wait_ge(logged, 1)
            nc.vector.scalar_tensor_tensor(m, d, 0.0, l, ALU.max, ALU.add)
            dve.drain()
            nc.vector.tensor_scalar(g.ln_lb, m, -1.0, None, ALU.mult)
            nc.vector.tensor_tensor(g.ln_1lb, d, m, ALU.subtract).then_inc(done, 1)

        @block.scalar
        def _(act):
            act.wait_ge(made, 1)
            nc.scalar.activation(a, d, ACT.Abs)
            act.drain()
            nc.scalar.activation(a, a, ACT.Exp, scale=-1.0)
            act.drain()
            nc.scalar.activation(l, a, ACT.Ln, bias=1.0).then_inc(logged, 1)


def forget_stage(nc, g, f, lf, u, y, write_after):
    with stage(nc, "fg", "l", "y", "yf", "k", "l2", "done") as (block, logged, y_ready, yf, k_ready, logged2, done):
        @block.scalar
        def _(act):
            for t in range(KD):
                nc.scalar.activation(u[:, t], f[:, t], ACT.Abs)
            act.drain()
            for t in range(KD):
                nc.scalar.activation(u[:, t], u[:, t], ACT.Exp, scale=-1.0)
            act.drain()
            for t in range(KD):
                nc.scalar.activation(u[:, t], u[:, t], ACT.Ln, bias=1.0).then_inc(logged, 1)
            for t in range(KD):
                act.wait_ge(yf, t + 1)
                nc.scalar.activation(f[:, t], f[:, t], ACT.Exp).then_inc(k_ready, 1)
                nc.scalar.activation(u[:, t], u[:, t], ACT.Abs)
            act.drain()
            for t in range(KD):
                nc.scalar.activation(u[:, t], u[:, t], ACT.Exp, scale=-1.0)
            act.drain()
            for t in range(KD):
                nc.scalar.activation(u[:, t], u[:, t], ACT.Ln, bias=1.0).then_inc(logged2, 1)

        @block.vector
        def _(dve):
            for t in range(KD):
                dve.wait_ge(logged, t + 1)
                nc.vector.scalar_tensor_tensor(y[:, t], f[:, t], 0.0, u[:, t], ALU.min, ALU.subtract).then_inc(y_ready, 1)
                dve.wait_ge(y_ready, 2 * t + 1)
                nc.vector.tensor_scalar(y[:, t], y[:, t], g.ln_1lb[:, t:t + 1], None, ALU.add).then_inc(y_ready, 1)
                dve.wait_ge(y_ready, 2 * t + 2)
                nc.vector.tensor_tensor(f[:, t], y[:, t], f[:, t], ALU.subtract)
                nc.vector.tensor_scalar(u[:, t], y[:, t], g.ln_lb[:, t:t + 1], None, ALU.subtract).then_inc(yf, 1)
            dve.wait_ge(*write_after)
            for t in range(KD):
                dve.wait_ge(logged2, t + 1)
                nc.vector.scalar_tensor_tensor(lf[:, t], y[:, t], g.ln_lb[:, t:t + 1], u[:, t], ALU.max, ALU.add).then_inc(done, 1)


def start_move(nc, moved, to, of):
    with nc.Block() as block:
        @block.sync
        def _(sp):
            sp.dma_start(to, of).then_inc(moved, 16)


def layer_one_mixer(nc, g, I):
    A = g.arena
    w = I["c_w_in_2"].rearrange("a k n -> (a k) n")
    by_tok = "(t p) d -> p t d"
    R0, R1, R2, R3, R4, R5 = (8192 * i for i in range(6))
    g.x, g.ht = A.at(R0, NT, D), A.at(R2, KD, T)
    g.w = [A.at(R1, KD, 512), A.at(R1 + 4096, KD, 512)]
    g.scratch = Arena_at(A, R3)
    x_out, gate_out, gate_in, x_in = g.moved
    start_loads(nc, g, (0, g.w[0], blocks_of(w, 3 * D, 512)(0)), (1, g.w[1], blocks_of(w, 3 * D, 512)(1)))
    start_move(nc, x_out, g.x_dram.rearrange(by_tok, p=P), g.x)
    norm_stage(nc, g, "n2", g.x, NT, D, g.ht, g.mix_g[:, 8:16])
    gate = A.at(R0, NT, D)
    q, f, v = A.at(R3, KD, T), A.at(R4, KD, T), A.at(R5, NT, D)
    feat = [by_feature(g.ht, j // 2, (j % 2) * 512, 512) for j in range(8)]
    tiles = [by_token(g.ht, t, 512) for t in range(NT)]

    def silu_feature(e, n, j, bank):
        return nc.scalar.activation(q[:, ds(n * 4 + j // 2, 1), (j % 2) * 512:(j % 2 + 1) * 512].rearrange("p a t -> p (a t)"), bank, ACT.Silu)

    def silu_token(e, n, j, bank):
        return nc.scalar.activation(gate[:, j, ds(n * 512, 512)], bank, ACT.Silu)

    project_pairs_scalar(nc, g, "gg", KD, tiles, blocks_of(w, 3 * D, 512), g.w, silu_token,
                         early=(0, 1), then=(g.w[0], blocks_of(w, 0, 512)(0)), write_after=(x_out, 16))
    start_move(nc, gate_out, g.gate_dram.rearrange(by_tok, p=P), gate)
    project_pairs_scalar(nc, g, "hq", KD, feat, blocks_of(w, 0, 512), g.w, silu_feature, early=(0,), then=(g.w[0], blocks_of(w, D, 512)(0)))
    project(nc, g, "hf", KD, feat, blocks_of(w, D, 512), 2, g.w,
            lambda e, n, j, bank: copy(nc, e, f[:, ds(n * 4 + j // 2, 1), (j % 2) * 512:(j % 2 + 1) * 512].rearrange("p a t -> p (a t)"), bank), early=(0,), then=(g.w[0], blocks_of(w, 2 * D, 512)(0)))
    project(nc, g, "hv", KD, tiles, blocks_of(w, 2 * D, 512), 2, g.w, lambda e, n, j, bank: copy(nc, e, v[:, j, ds(n * 512, 512)], bank), early=(0,))
    lf = A.at(R0, KD, T)
    lower_bound_stage(nc, g)
    forget_stage(nc, g, f, lf, A.at(R1, KD, T), A.at(R2, KD, T), (gate_out, 16))
    gated_stage(nc, g, I, "hgrn", KD, 1, q, f, lf, v, P ** -0.5, Arena_at(A, R1))
    gate = A.at(R4, NT, D)
    start_move(nc, gate_in, gate, g.gate_dram.rearrange(by_tok, p=P))
    start_move(nc, x_in, g.x, g.x_dram.rearrange(by_tok, p=P))
    w_c = I["c_w_out_2"].rearrange("a k n -> (a k) n")
    head_norm_stage(nc, g, I, "hn", v, HEADS * 2, I["hgrn_norm_g_2"].rearrange("a n -> (a n)"), gate, Arena_at(A, R1), (gate_in, 16))
    start_loads(nc, g, (0, g.w[0], blocks_of(w_c, 0, 512)(0)), (1, g.w[1], blocks_of(w_c, 0, 512)(1)))
    ot = A.at(R3, KD, T)
    transpose_stage(nc, g, "hot", gate, ot)
    g.scratch = Arena_at(A, R4)
    out_proj(nc, g, "co", ot, w_c, early=(0, 1), x_after=(x_in, 16))


def project_pairs_scalar(nc, g, name, K, groups, w_src, wbufs, evac, early=(), then=None, write_after=None):
    G = len(groups)
    early_by = [(b, g.n_early[b]) for b in early]
    with stage(nc, name, "w0", "w1", "mm", "ev") as (block, w0, w1, mm, ev):
        landed = (w0, w1)

        @block.sync
        def _(sp):
            for b in range(2):
                if b not in early:
                    sp.dma_start(wbufs[b], w_src(b)).then_inc(landed[b], 16)
            if then is not None:
                sp.wait_ge(mm, G)
                sp.dma_start(*then).then_inc(g.early[0], 16)

        @block.tensor
        def _(pe):
            for b, n in early_by:
                pe.wait_ge(g.early[b], n)
            for b in range(2):
                if b not in early:
                    pe.wait_ge(landed[b], 16)
                for j in range(G):
                    if b:
                        pe.wait_ge(ev, j + 1)
                    for k in range(K):
                        lhsT, rhs, out = groups[j](wbufs[b], k, g.ps[:, j, :])
                        last = nc.tensor.matmul(out, lhsT, rhs, start=(k == 0), stop=(k == K - 1))
                    last.then_inc(mm, 1)

        @block.scalar
        def _(act):
            if write_after is not None:
                act.wait_ge(*write_after)
            for b in range(2):
                for j in range(G):
                    act.wait_ge(mm, b * G + j + 1)
                    evac(1, b, j, g.ps[:, j, :]).then_inc(ev, 1)
    if then is not None:
        g.n_early[0] += 16


def router_stage(nc, g, I):
    S = g.scratch
    wr = S.at(0, KD, NE)
    lg, mask, ex = S.at(64, NT, NE), S.at(128, NT, NE), S.at(192, NT, NE)
    top, ti = S.at(256, NT, 8), S.at(320, NT, 8).bitcast(U32)
    tif = S.at(384, NT, 2)
    onehot = S.at(400, NT, 2, NE)
    posf, tmp = S.at(528, NT, 2), S.at(544, NT, NE)
    iota8, cnt, nu, cum, first = S.at(608, NE), S.at(616, NE), S.at(624, NE), S.at(632, NE), S.at(640, NE)
    iu, row, eidx, cnt_u, vu = S.at(656, MAX_UNITS), S.at(672, MAX_UNITS, NE), S.at(768, MAX_UNITS), S.at(784, MAX_UNITS), S.at(800, MAX_UNITS)
    row2, tot = S.at(816, MAX_UNITS, NE), S.at(912, 2)
    w12, gr, zero_i = S.at(920, NT, 2), S.at(936, MAX_UNITS, 8), S.at(1032, SLOTS // P).bitcast(U32)
    steps_of, past = S.at(1100, UNIT // GRAIN - 1), S.at(1140, MAX_UNITS, UNIT // GRAIN - 1)
    tok_i = g.tok_ids
    with stage(nc, "route", "in", "mm", "exp", "top", "cnt", "tab", "pos", "iota", "zero", "scat", "done", "ids") as (block, arrived, mm, exped, topped, counted, tabled, placed, iotas, zeroed, scattered, done, ids):
        @block.sync
        def _(sp):
            sp.dma_start(wr, I["moe_router_2"].rearrange("a (k p) e -> p (a k) e", p=P)).then_inc(arrived, 16)
            sp.wait_ge(zeroed, 1)
            sp.dma_start(g.slot_dram.rearrange("(p n) a -> p (n a)", p=P), zero_i).then_inc(scattered, 16)

        @block.gpsimd
        def _(pool):
            nc.gpsimd.iota(iota8, [[1, NE]], base=0, channel_multiplier=0, allow_small_or_imprecise_dtypes=True)
            nc.gpsimd.iota(iu, [[1, MAX_UNITS]], base=0, channel_multiplier=0, allow_small_or_imprecise_dtypes=True)
            nc.gpsimd.iota(steps_of, [[GRAIN, UNIT // GRAIN - 1]], base=GRAIN, channel_multiplier=0, allow_small_or_imprecise_dtypes=True)
            nc.gpsimd.iota(tok_i, [[P, NT]], base=0, channel_multiplier=1)
            pool.drain().then_inc(iotas, 1)
            pool.wait_ge(placed, 1)
            pool.wait_ge(scattered, 16)
            for t in range(NT):
                for a in range(2):
                    nc.gpsimd.indirect_dma_start(g.slot_dram, bass.IndirectOffsetOnAxis(ap=g.pos[:, t, a:a + 1], axis=0), tok_i[:, t:t + 1], None,
                                                 bounds_check=SLOTS - 1, oob_is_err=False).then_inc(ids, 16)
            pool.wait_ge(ids, 16 * 2 * NT)

        @block.tensor
        def _(pe):
            pe.wait_ge(arrived, 16)
            for t in range(NT):
                for k in range(KD):
                    last = nc.tensor.matmul(g.ps[:, 0, t * NE:(t + 1) * NE], g.ht[:, k, t * P:(t + 1) * P], wr[:, k, :], start=(k == 0), stop=(k == KD - 1))
            last.then_inc(mm, 1)
            pe.wait_ge(topped, 1)
            for t in range(NT):
                for b in range(t):
                    nc.tensor.matmul(g.ps[:, 1, t * NE:(t + 1) * NE], g.ones, mask[:, b, :], start=(b == 0), stop=False)
                nc.tensor.matmul(g.ps[:, 1, t * NE:(t + 1) * NE], g.tri, mask[:, t, :], start=(t == 0), stop=True)
            for b in range(NT):
                last = nc.tensor.matmul(g.ps[:, 2, 0:NE], g.ones, mask[:, b, :], start=(b == 0), stop=(b == NT - 1))
            last.then_inc(counted, 1)

        @block.scalar
        def _(act):
            act.wait_ge(exped, 1)
            nc.scalar.activation(w12[:, :, 1], tmp[:, :, 0], ACT.Exp).then_inc(exped, 1)

        @block.vector
        def _(dve):
            v = nc.vector

            def step(x):
                x
                dve.drain()

            v.memset(zero_i, 0).then_inc(zeroed, 1)
            dve.wait_ge(mm, 1)
            dve.wait_ge(iotas, 1)
            step(v.tensor_copy(lg, g.ps[:, 0, 0:NT * NE].rearrange("p (t e) -> p t e", e=NE)))
            for t in range(NT):
                step(v.max(top[:, t, :], lg[:, t, :]))
                step(v.max_index(ti[:, t, :], top[:, t, :], lg[:, t, :]))
            step(v.tensor_copy(tif, ti[:, :, 0:2]))
            for t in range(NT):
                v.tensor_tensor(onehot[:, t], iota8.unsqueeze(1).broadcast_to([P, 2, NE]), tif[:, t, :].unsqueeze(2).broadcast_to([P, 2, NE]), ALU.is_equal)
            dve.drain()
            v.tensor_tensor(mask, onehot[:, :, 0, :], onehot[:, :, 1, :], ALU.add).then_inc(topped, 1)
            v.tensor_tensor(tmp[:, :, 0], top[:, :, 1], top[:, :, 0], ALU.subtract).then_inc(exped, 1)
            dve.wait_ge(exped, 2)
            step(v.tensor_scalar(w12[:, :, 0], w12[:, :, 1], 1.0, None, ALU.add))
            step(v.reciprocal(g.gk[:, :, 0], w12[:, :, 0]))
            step(v.tensor_tensor(g.gk[:, :, 1], g.gk[:, :, 0], w12[:, :, 1], ALU.mult))
            dve.wait_ge(counted, 1)
            step(v.tensor_copy(cnt, g.ps[:, 2, 0:NE]))
            step(v.tensor_scalar(nu, cnt, 0.0, None, ALU.is_gt))
            for i in range(1, T // UNIT):
                step(v.scalar_tensor_tensor(nu, cnt, float(i * UNIT), nu, ALU.is_gt, ALU.add))
            step(v.tensor_tensor_scan(cum, g.ones[:, 0:NE], nu, 0.0, ALU.mult, ALU.add))
            step(v.tensor_tensor(first, cum, nu, ALU.subtract))
            step(v.tensor_tensor(row, cum.unsqueeze(1).broadcast_to([P, MAX_UNITS, NE]), iu.unsqueeze(2).broadcast_to([P, MAX_UNITS, NE]), ALU.is_le))
            step(v.tensor_reduce(eidx, row, AX.X, ALU.add))
            step(v.tensor_tensor(row, iota8.unsqueeze(1).broadcast_to([P, MAX_UNITS, NE]), eidx.unsqueeze(2).broadcast_to([P, MAX_UNITS, NE]), ALU.is_equal))
            step(v.scalar_tensor_tensor(tmp[:, 0, :], first, float(UNIT), cnt, ALU.mult, ALU.add))
            step(v.tensor_tensor(row2, row, tmp[:, 0, :].unsqueeze(1).broadcast_to([P, MAX_UNITS, NE]), ALU.mult))
            step(v.tensor_reduce(cnt_u, row2, AX.X, ALU.add))
            step(v.scalar_tensor_tensor(cnt_u, iu, -float(UNIT), cnt_u, ALU.mult, ALU.add))
            step(v.tensor_tensor(past, cnt_u.unsqueeze(2).broadcast_to([P, MAX_UNITS, UNIT // GRAIN - 1]), steps_of.unsqueeze(1).broadcast_to([P, MAX_UNITS, UNIT // GRAIN - 1]), ALU.is_gt))
            step(v.tensor_reduce(vu, past, AX.X, ALU.add))
            step(v.tensor_scalar(vu, vu, 1.0, None, ALU.add))
            step(v.tensor_scalar(eidx, eidx, float(NE - 1), None, ALU.min))
            step(v.tensor_copy(g.table[:, 0, :], eidx))
            step(v.tensor_copy(g.table[:, 1, :], vu))
            step(v.tensor_copy(g.n_units, cum[:, NE - 1:NE]))
            step(v.scalar_tensor_tensor(ex, first.unsqueeze(1).broadcast_to([P, NT, NE]), float(UNIT), g.ps[:, 1, 0:NT * NE].rearrange("p (t e) -> p t e", e=NE), ALU.mult, ALU.add))
            for a in range(2):
                step(v.tensor_tensor(tmp, ex, onehot[:, :, a, :], ALU.mult))
                step(v.tensor_reduce(posf[:, :, a], tmp, AX.X, ALU.add))
            v.tensor_copy(g.pos, posf).then_inc(placed, 1)


def expert_stage(nc, g, I, A, write_after):
    UK, UE = KD, EF_T
    NB_UP, NB_DN = E_FF // 256, D // P
    xg = A.at(0, 4, D)
    xt = A.at(4096, KD, UNIT)
    hid = A.at(8192, EF_T, UNIT)
    yt = A.at(22528, KD, UNIT)
    yg = A.at(26624, 4, D)
    wup = [A.at(30720 + 4096 * i, KD, 512) for i in range(2)]
    wdn = [A.at(38912 + 3584 * i, EF_T, P) for i in range(2)]
    sg = A.at(46080, 4, UNIT)
    idx = g.idx
    wg_v = I["moe_w_gate_2"].rearrange("a e (k p) n -> p (a e) k n", p=P)
    wu_v = I["moe_w_up_2"].rearrange("a e (k p) n -> p (a e) k n", p=P)
    wd_v = I["moe_w_down_2"].rearrange("a e (f p) n -> p (a e) f n", p=P)
    sems = ("u0", "u1", "d0", "d1", "ix", "xg", "xt_tr", "xt", "up", "sg", "hid", "dn", "yt", "yt_tr", "yg", "yout", "zero")
    with stage(nc, "moe", *sems) as (block, u0, u1, d0, d1, ix, xgot, turned, xt_ready, up_done, silu, hidden, dn_done, yt_ready, y_turned, yg_ready, y_out, zeroed):
        up_in, dn_in = (u0, u1), (d0, d1)

        def units(eng):
            return eng.value_load(g.n_units[0:1, 0:1], min_val=1, max_val=MAX_UNITS)

        @block.sync
        def _(sp):
            n = units(sp)
            with sp.Fori(0, n) as u:
                e = sp.value_load(g.table[0:1, 0, ds(u, 1)], min_val=0, max_val=NE - 1)

                def load_up(i, b):
                    for a, w in enumerate((wg_v, wu_v)):
                        sp.dma_start(wup[b][:, :, a * 256:(a + 1) * 256], w[:, ds(e, 1), :, ds(i * 256, 256)].rearrange("p e k n -> p (e k) n")).then_inc(up_in[b], 16)

                def load_dn(i, b):
                    sp.dma_start(wdn[b], wd_v[:, ds(e, 1), :, ds(i * P, P)].rearrange("p e k n -> p (e k) n")).then_inc(dn_in[b], 16)

                with sp.Fori(0, NB_UP // 2) as i:
                    for b in range(2):
                        sp.wait_ge(up_done, u * (2 * NB_UP) + i * 4 + (2 * b + 1))
                        load_up(i * 2 + b, b)
                with sp.Fori(0, NB_DN // 2) as i:
                    for b in range(2):
                        sp.wait_ge(dn_done, u * NB_DN + i * 2 + (b + 1))
                        load_dn(i * 2 + b, b)

        @block.gpsimd
        def _(pool):
            n = units(pool)
            pool.wait_ge(*write_after)
            with pool.Fori(0, n) as u:
                pool.wait_ge(turned, u * 4 + 1)
                pool.wait_ge(zeroed, 1)
                pool.dma_start(idx, g.slot_dram.rearrange("(u p b) a -> p u (b a)", b=4, p=P)[:, ds(u, 1), :].rearrange("p u b -> p (u b)")).then_inc(ix, 16)
                pool.wait_ge(ix, u * 16 + 16)
                nc.gpsimd.tensor_tensor(g.mark[:, 1:2], g.ones[:, 0:1], g.ones[:, 0:1], ALU.mult)
                pool.drain()
                for b in range(4):
                    nc.gpsimd.indirect_dma_start(xg[:, b, :], None, g.h_dram, bass.IndirectOffsetOnAxis(ap=idx[:, b:b + 1], axis=0),
                                                 bounds_check=T - 1, oob_is_err=False).then_inc(xgot, 16)
                pool.wait_ge(xgot, u * 64 + 64)

        @block.vector
        def _(dve):
            n = units(dve)
            for b in range(8):
                last = nc.vector.memset(g.ps[:, b, :], 0.0)
            last.then_inc(zeroed, 1)
            credit(dve, hidden, 2)
            credit(dve, xt_ready, 2)
            credit(dve, yg_ready, 2)
            with dve.Fori(0, n) as u:
                for b in range(4):
                    dve.wait_ge(turned, u * 4 + (b + 2))
                    nc.vector.tensor_tensor(xt.rearrange("p k (t b) -> p b k t", b=4)[:, b], g.ps[:, 2 * (b % 2):2 * (b % 2) + 2, :].rearrange("p a (k t) -> p (a k) t", t=P),
                                            g.ffn_g[:, 8:16].unsqueeze(2).broadcast_to([P, KD, P]), ALU.mult).then_inc(xt_ready, 1)
                with dve.Fori(0, EF_T // 2) as i:
                    for b in range(2):
                        dve.wait_ge(silu, u * EF_T + i * 2 + (b + 1))
                        nc.vector.tensor_tensor(hid[:, ds(i * 2 + b, 1), :].rearrange("p a t -> p (a t)"), sg[:, b, :], g.ps[:, 2 * b + 1, :], ALU.mult).then_inc(hidden, 1)
                for b in range(4):
                    dve.wait_ge(y_turned, u * 4 + (b + 1))
                    dve.wait_ge(y_out, u * 16 + 16)
                    nc.vector.tensor_copy(yg[:, b, :], g.ps[:, 6 - 2 * (b % 2):8 - 2 * (b % 2), :].rearrange("p a n -> p (a n)")).then_inc(yg_ready, 1)

        @block.scalar
        def _(act):
            n = units(act)
            credit(act, y_out, 16)
            act.wait_ge(g.y_cleared, 16)
            credit(act, yt_ready, 2)
            with act.Fori(0, n) as u:
                with act.Fori(0, EF_T // 2) as i:
                    for b in range(2):
                        act.wait_ge(up_done, u * EF_T + i * 2 + (b + 4))
                        act.wait_ge(hidden, u * EF_T + i * 2 + (b + 1))
                        nc.scalar.activation(sg[:, b, :], g.ps[:, 2 * b, :], ACT.Silu).then_inc(silu, 1)
                with act.Fori(0, NB_DN // 2) as i:
                    for b in range(2):
                        act.wait_ge(dn_done, u * NB_DN + i * 2 + (b + 3))
                        nc.scalar.activation(yt[:, ds(i * 2 + b, 1), :].rearrange("p a t -> p (a t)"), g.ps[:, 4 + b, :], ACT.Copy).then_inc(yt_ready, 1)
                act.wait_ge(yg_ready, u * 4 + 6)
                act.dma_start(g.y_dram.rearrange("(u b p) d -> p u b d", b=4, p=P)[:, ds(u, 1), :, :].rearrange("p u b d -> p (u b) d"), yg).then_inc(y_out, 16)
            act.wait_ge(y_out, n * 16 + 16)
            nc.scalar.activation(g.mark[:, 2:3], g.ones[:, 0:1], ACT.Copy)

        @block.tensor
        def _(pe):
            n = units(pe)
            credit(pe, up_done, 3)
            credit(pe, dn_done, 2)
            credit(pe, turned, 1)
            pe.wait_ge(zeroed, 1)
            with pe.Fori(0, n) as u:
                grains = pe.value_load(g.table[0:1, 1, ds(u, 1)], min_val=1, max_val=UNIT // GRAIN)
                pe.wait_ge(xgot, u * 64 + 64)
                for b in range(4):
                    pe.wait_ge(xt_ready, u * 4 + (b + 1))
                    for k in range(KD):
                        last = nc.tensor.transpose(g.ps[:, 2 * (b % 2) + k // 4, (k % 4) * P:(k % 4 + 1) * P], xg[:, b, k * P:(k + 1) * P], g.ident)
                    last.then_inc(turned, 1)
                pe.wait_ge(xt_ready, u * 4 + 6)
                pe.wait_ge(yg_ready, u * 4 + 2)
                for v in range(1, UNIT // GRAIN + 1):
                    N = v * GRAIN
                    with pe.If(grains == v):
                        with pe.Fori(0, NB_UP // 2) as i:
                            for b in range(2):
                                pe.wait_ge(up_in[b], u * (NB_UP // 2 * 32) + i * 32 + 32)
                                for f in range(2):
                                    pe.wait_ge(hidden, u * EF_T + i * 4 + (2 * b + f + 1))
                                    for a in range(2):
                                        for k in range(KD):
                                            last = nc.tensor.matmul(g.ps[:, 2 * f + a, 0:N], wup[b][:, k, a * 256 + f * P:a * 256 + (f + 1) * P], xt[:, k, 0:N],
                                                                    start=(k == 0), stop=(k == KD - 1))
                                    last.then_inc(up_done, 1)
                        with pe.Fori(0, NB_DN // 2) as i:
                            for b in range(2):
                                pe.wait_ge(dn_in[b], u * (NB_DN // 2 * 16) + i * 16 + 16)
                                pe.wait_ge(hidden, u * EF_T + (EF_T + 2))
                                pe.wait_ge(yt_ready, u * NB_DN + i * 2 + (b + 1))
                                for k in range(EF_T):
                                    last = nc.tensor.matmul(g.ps[:, 4 + b, 0:N], wdn[b][:, k, :], hid[:, k, 0:N], start=(k == 0), stop=(k == EF_T - 1))
                                last.then_inc(dn_done, 1)
                pe.wait_ge(yt_ready, u * NB_DN + (NB_DN + 2))
                for b in range(4):
                    pe.wait_ge(yg_ready, u * 4 + (b + 1))
                    for k in range(KD):
                        last = nc.tensor.transpose(g.ps[:, 6 - 2 * (b % 2) + k // 4, (k % 4) * P:(k % 4 + 1) * P], yt[:, k, b * P:(b + 1) * P], g.ident)
                    last.then_inc(y_turned, 1)


def combine_stage(nc, g, I, out, A):
    x = A.at(0, NT, D)
    y = [A.at(8192 + 2048 * i, 2, D) for i in range(4)]
    grow = A.at(16384, D)
    junk = A.at(17408, D)
    res = A.at(18432, NT, D)
    ss, sq, rs = g.small.at(0, NT), g.small.at(16, NT), g.small.at(32, NT)
    with stage(nc, "comb", "x", "y0", "y1", "y2", "y3", "sum", "root", "res", "out") as (block, x_in, y0, y1, y2, y3, summed, root, ready, stored):
        y_in = (y0, y1, y2, y3)

        @block.sync
        def _(sp):
            sp.dma_start(x, g.x_dram.rearrange("(t p) d -> p t d", p=P)).then_inc(x_in, 16)
            sp.dma_start(grow, rows(I["final_norm_g_2"])).then_inc(x_in, 16)
            for t in range(NT):
                sp.wait_ge(ready, t + 1)
                sp.dma_start(out[0, t * P:(t + 1) * P, :], res[:, t, :]).then_inc(stored, 16)
            sp.wait_ge(stored, 16 * NT)

        @block.gpsimd
        def _(pool):
            for t in range(NT):
                if t >= 4:
                    pool.wait_ge(summed, t - 3)
                for a in range(2):
                    nc.gpsimd.indirect_dma_start(y[t % 4][:, a, :], None, g.y_dram, bass.IndirectOffsetOnAxis(ap=g.pos[:, t, a:a + 1], axis=0),
                                                 bounds_check=SLOTS - 1, oob_is_err=False).then_inc(y_in[t % 4], 16)

        @block.vector
        def _(dve):
            dve.wait_ge(x_in, 32)

            def add(t):
                dve.wait_ge(y_in[t % 4], 32 * (t // 4 + 1))
                nc.vector.scalar_tensor_tensor(x[:, t], y[t % 4][:, 0, :], g.gk[:, t, 0:1], x[:, t], ALU.mult, ALU.add)
                dve.drain()
                nc.vector.scalar_tensor_tensor(x[:, t], y[t % 4][:, 1, :], g.gk[:, t, 1:2], x[:, t], ALU.mult, ALU.add).then_inc(summed, 1)

            def scale(t):
                dve.wait_ge(root, t + 1)
                nc.vector.reciprocal(rs[:, t:t + 1], sq[:, t:t + 1])
                dve.drain()
                nc.vector.scalar_tensor_tensor(res[:, t, :], x[:, t], rs[:, t:t + 1], grow, ALU.mult, ALU.mult).then_inc(ready, 1)

            add(0)
            for t in range(NT):
                if t + 1 < NT:
                    add(t + 1)
                scale(t)

        @block.scalar
        def _(act):
            for t in range(NT):
                act.wait_ge(summed, t + 1)
                nc.scalar.activation(junk, x[:, t], ACT.Square, accum_out=ss[:, t:t + 1])
                act.drain()
                nc.scalar.activation(sq[:, t:t + 1], ss[:, t:t + 1], ACT.Sqrt, scale=1.0 / D, bias=g.eps[:, 0:1]).then_inc(root, 1)



def experts(nc, g, I, out):
    A = g.arena
    g.scratch = Arena_at(A, 32768)
    g.ht = A.at(16384, KD, T)
    norm_stage(nc, g, "n3", g.x, NT, D, g.ht, g.ffn_g[:, 8:16], rows_out=g.h_dram)
    x_out2 = nc.alloc_semaphore("moved_x_out2")
    start_move(nc, x_out2, g.x_dram.rearrange("(t p) d -> p t d", p=P), g.x)
    router_stage(nc, g, I)
    expert_stage(nc, g, I, A, (x_out2, 16))
    combine_stage(nc, g, I, out, A)


class Places:
    pass


def first_block(nc, g, I):
    A = g.arena
    g.x = A.at(0, NT, D)
    g.w = [A.at(8192, KD, 512), A.at(12288, KD, 512)]
    g.ht = A.at(16384, KD, KEYS)
    g.lr = A.at(26624, NK, LR)
    g.br = A.at(31104, NT, D)
    g.pt = A.at(39296, 4, T + PAD)
    g.scratch = Arena_at(A, 43520)
    g.ctx = A.at(26624, NC_T, D)
    load_stage(nc, g, I)
    mod_stage(nc, g, I)
    start_loads(nc, g, (0, g.w[0][:, :, 0:LR], blocks_of(I["w_in"].rearrange("a k n -> (a k) n"), 0, LR)(0)),
                (1, g.w[1], blocks_of(I["w_in"].rearrange("a k n -> (a k) n"), LR, 512)(0)))
    norm_stage(nc, g, "nx", g.x, NT, D, g.ht, g.a1[:, 0, :], g.b1[:, 0, :])
    norm_stage(nc, g, "nctx", g.ctx, NC_T, D, g.ht[:, :, T:KEYS], g.a1[:, 1, :], g.b1[:, 1, :])
    in_proj_stages(nc, g, I)
    pool_stage(nc, g, I)
    g.scratch = Arena_at(A, 39296)
    g.cqt = A.at(43520, 2, T)
    g.ckvt = A.at(45568, KEYS)
    g.krt = A.at(46848, NK, ROPE)
    lora_norm_stage(nc, g)
    g.qt = A.at(16384, HEADS, T)
    g.kt = A.at(20480, HEADS, KEYS)
    g.kr = A.at(26624, 2, KEYS)
    g.v = A.at(8192, NK, 512)
    g.w_small = Arena_at(A, 13312)
    g.qr = A.at(47488, 2, T)
    with stage(nc, "axial", "in") as (block, arrived):
        @block.sync
        def _(sp):
            for i in range(2):
                sp.dma_start(g.axial[:, i, :, :], I["axial"][i].rearrange("(t p) r -> p t r", p=P)).then_inc(arrived, 16)
            sp.wait_ge(arrived, 32)
    head_stage(nc, g, I, "qh", NT, 2, HEADS * QK, lambda k, t: g.cqt[:, k, t * P:(t + 1) * P], I["w_uq"], g.qt, g.qr, I["q_norm_g"], False)
    head_stage(nc, g, I, "kh", NK, 1, HEADS * 256, lambda k, t: g.ckvt[:, t * P:(t + 1) * P], I["w_ukv"], g.kt, g.kr, I["k_norm_g"], True)
    g.p = A.at(39296, 2, KEYS)
    g.ptb = A.at(41856, KEYS)
    attention_stage(nc, g)
    g.brt = A.at(16384, KD, T)
    w_out = blocks_of(I["w_out"].rearrange("a k n -> (a k) n"), 0, 512)
    start_loads(nc, g, (0, g.w[0], w_out(0)), (1, g.w[1], w_out(1)))
    transpose_stage(nc, g, "brt", g.br, g.brt)
    g.scratch = Arena_at(A, 43520)
    out_proj(nc, g, "wout", g.brt, I["w_out"].rearrange("a k n -> (a k) n"), g.gate_row, early=(0, 1))


def Arena_at(arena, off):
    a = Arena(arena.t[:, off:])
    return a


def program(nc, I, out):
    with ExitStack() as cx:
        def sb(name, *shape, dt=F32):
            return cx.enter_context(nc.sbuf_tensor(name, [P, *shape], dt))

        g = Places()
        arena = sb("arena", 49600)
        g.arena = Arena(arena)
        psum = cx.enter_context(nc.psum_tensor("psum", [P, 8, 512], F32))
        g.ps = psum
        g.ident = sb("ident", P)[:, :]
        g.tri = sb("tri", P)[:, :]
        g.ones = sb("ones", P)[:, :]
        g.eps = sb("eps", 1)
        g.small = Arena(sb("small", 96))
        g.vec = sb("vec", VECS)[:, :]
        g.b_mod, g.norm_g, g.lora_g = g.vec[:, 16:40], g.vec[:, 40:48], g.vec[:, 48:51]
        g.mix_g, g.ffn_g, g.lb, g.ba2 = g.vec[:, 51:67], g.vec[:, 67:83], g.vec[:, 83:99], g.vec[:, 99:101]
        g.cs, g.mod = sb("cs", KD, 2)[:, :, :], sb("mod", 24, 2)[:, :, :]
        g.a1, g.b1 = sb("a1", 2, KD)[:, :, :], sb("b1", 2, KD)[:, :, :]
        g.gate_row = sb("gate_row", D)[:, :]
        g.axial = sb("axial", 2, NT, ROPE)[:, :, :, :]
        g.norm_row = sb("norm_row", QK)[:, :]
        g.qs = sb("qs", 1)[:, :]
        g.mark = sb("mark", 3)[:, :]
        g.zeros = sb("zeros", ZERO_W)[:, :]
        g.y_cleared = nc.alloc_semaphore("y_cleared")
        g.early, g.n_early = [nc.alloc_semaphore(f"early{b}") for b in range(2)], [0, 0]
        g.moved = [nc.alloc_semaphore(f"moved_{n}") for n in ("x_out", "gate_out", "gate_in", "x_in")]
        g.ln_lb, g.ln_1lb = sb("ln_lb", KD)[:, :], sb("ln_1lb", KD)[:, :]
        g.pos, g.gk = sb("pos", NT, 2, dt=U32)[:, :, :], sb("gk", NT, 2)[:, :, :]
        g.tok_ids, g.idx = sb("tok_ids", NT, dt=U32)[:, :], sb("idx", 4, dt=U32)[:, :]
        g.table, g.n_units = sb("table", 2, MAX_UNITS, dt=I32)[:, :, :], sb("n_units", 1, dt=I32)[:, :]
        g.x_dram = nc.dram_tensor("x_dram", (T, D), F32).ap()
        g.gate_dram = nc.dram_tensor("gate_dram", (T, D), F32).ap()
        g.h_dram = nc.dram_tensor("h_dram", (T, D), F32).ap()
        g.y_dram = nc.dram_tensor("y_dram", (SLOTS, D), F32).ap()
        g.slot_dram = nc.dram_tensor("slot_dram", (SLOTS, 1), U32).ap()
        first_block(nc, g, I)
        layer_zero(nc, g, I)
        layer_one_mixer(nc, g, I)
        experts(nc, g, I, out)


def kernel(**inputs):
    from concourse import bacc
    from concourse.bass_utils import run_bass_kernel_spmd

    nc = bacc.Bacc("TRN2", target_bir_lowering=False, num_devices=1)
    arrays, I = {}, {}
    for name, value in {**inputs, **shape_constants()}.items():
        a = np.ascontiguousarray(value)
        arrays[f"in_{name}"] = a
        I[name] = nc.dram_tensor(f"in_{name}", a.shape, mybir.dt.from_np(a.dtype), kind="ExternalInput").ap()
    out = nc.dram_tensor("out", (1, T, D), F32, kind="ExternalOutput").ap()
    program(nc, I, out)
    return run_bass_kernel_spmd(nc, [arrays], core_ids=[0]).results[0]["out"]
```
